# Optimizing a Trainium2 kernel written in Bass

```python
import math
import jax
import jax.numpy as jnp
from jax import lax
import numpy as np

D_MODEL = 1024
BATCH = 1
SEQ = 512
DEPTH = 1

NORM_EPS = 1e-6
NEG_INF = -1e30
TOP_BONUS = 1e9
NUM_BUCKETS = 32
T5_MAX_DISTANCE = 128
NSA_HEADS = 8
NSA_KV_GROUPS = 2
NSA_HEAD_DIM = 64
CMP_LEN = 32
CMP_STRIDE = 16
SEL_BLOCK = 64
SEL_TOPK = 16
WINDOW = 512
NSA_Q_BLOCK = 128
NSA_WIDTH = NSA_HEADS * NSA_HEAD_DIM
NSA_KV_WIDTH = NSA_KV_GROUPS * NSA_HEAD_DIM
N_NSA_BRANCH = 3
GLA_HEADS = 4
GLA_KEY_DIM = 64
GLA_VAL_DIM = 128
GLA_GATE_RANK = 16
GLA_GATE_TAU = 16.0
GLA_CHUNK = 64
MOBA_HEADS = 8
MOBA_HEAD_DIM = 64
MOBA_BLOCK = 256
MOBA_TOPK = 3
MOBA_Q_BLOCK = 32
MOBA_WIDTH = MOBA_HEADS * MOBA_HEAD_DIM
N_BRANCHES = 3
FFN_HIDDEN = ((8 * D_MODEL + 3 * 256 - 1) // (3 * 256)) * 256
SPLIT_SIZES = (
    NSA_WIDTH,
    NSA_KV_WIDTH, NSA_KV_WIDTH,
    NSA_KV_WIDTH, NSA_KV_WIDTH,
    NSA_KV_WIDTH, NSA_KV_WIDTH,
    NSA_HEADS * N_NSA_BRANCH,
    GLA_HEADS * GLA_KEY_DIM, GLA_HEADS * GLA_KEY_DIM, GLA_HEADS * GLA_VAL_DIM, GLA_HEADS * GLA_VAL_DIM, GLA_GATE_RANK,
    MOBA_WIDTH, MOBA_WIDTH, MOBA_WIDTH,
    N_BRANCHES * D_MODEL,
)
D_IN = sum(SPLIT_SIZES)

kernel_name = 'hybrid_nsa_gla_moba_block'

def rmsnorm(x, w):
    xf = x.astype(jnp.float32)
    y = xf * lax.rsqrt(jnp.mean(xf * xf, axis=-1, keepdims=True) + NORM_EPS)
    return (y * w.astype(jnp.float32)).astype(x.dtype)

def t5_bucket(dist):
    n = jnp.maximum(dist, 0)
    max_exact = NUM_BUCKETS // 2
    log_ratio = jnp.log(jnp.maximum(n, 1).astype(jnp.float32) / max_exact) / math.log(T5_MAX_DISTANCE / max_exact)
    large = max_exact + (log_ratio * (NUM_BUCKETS - max_exact)).astype(jnp.int32)
    return jnp.where(n < max_exact, n, jnp.minimum(large, NUM_BUCKETS - 1))

def masked_softmax(s, mask):
    s = jnp.where(mask, s.astype(jnp.float32), NEG_INF)
    m = jnp.max(s, axis=-1, keepdims=True)
    e = jnp.where(mask, jnp.exp(s - m), 0.0)
    return e / jnp.maximum(jnp.sum(e, axis=-1, keepdims=True), 1e-20)

def split_heads(t, n_heads):
    b, s, _ = t.shape
    return t.reshape(b, s, n_heads, -1).transpose(0, 2, 1, 3)

def compress(t, pe, w1, w2):
    b, g, s, d = t.shape
    ratio = CMP_LEN // CMP_STRIDE
    n_cmp = (s - CMP_LEN) // CMP_STRIDE + 1
    pieces = t.reshape(b, g, s // CMP_STRIDE, CMP_STRIDE, d)
    blocks = jnp.concatenate([pieces[:, :, m:m + n_cmp] for m in range(ratio)], axis=3)
    flat = (blocks + pe).reshape(b, g, n_cmp, CMP_LEN * d)
    return jax.nn.gelu(flat @ w1) @ w2

def nsa_mixer(q, kc, vc, ks, vs, kw, vw, gates, rel_a, pe_k, pe_v, ck_w1, ck_w2, cv_w1, cv_w2):
    b, s, _ = q.shape
    G, R, dk = NSA_KV_GROUPS, NSA_HEADS // NSA_KV_GROUPS, NSA_HEAD_DIM
    qh = q.reshape(b, s, G, R, dk).transpose(0, 2, 3, 1, 4) * dk ** -0.5
    gh = jax.nn.sigmoid(gates).reshape(b, s, G, R, N_NSA_BRANCH).transpose(0, 2, 3, 1, 4)
    kc, vc, ks, vs, kw, vw = [split_heads(t, G) for t in (kc, vc, ks, vs, kw, vw)]
    k_cmp = compress(kc, pe_k, ck_w1, ck_w2)
    v_cmp = compress(vc, pe_v, cv_w1, cv_w2)
    n_cmp = k_cmp.shape[2]
    cmp_end = jnp.arange(n_cmp) * CMP_STRIDE + CMP_LEN - 1
    cmp_start = cmp_end - (CMP_LEN - 1)
    n_sb = s // SEL_BLOCK
    n_sel = min(SEL_TOPK, n_sb)
    sb_start = jnp.arange(n_sb) * SEL_BLOCK
    overlap = ((cmp_start[:, None] < sb_start[None, :] + SEL_BLOCK) & (cmp_end[:, None] >= sb_start[None, :])).astype(jnp.float32)
    ks_blk = ks.reshape(b, G, n_sb, SEL_BLOCK, dk)
    vs_blk = vs.reshape(b, G, n_sb, SEL_BLOCK, dk)
    pad = ((0, 0), (0, 0), (WINDOW, 0), (0, 0))
    kw_pad = jnp.pad(kw, pad)
    vw_pad = jnp.pad(vw, pad)
    rel_g = rel_a.reshape(NUM_BUCKETS, G, R)
    bi = jnp.arange(b)[:, None, None, None]
    gi = jnp.arange(G)[None, :, None, None]
    Q = NSA_Q_BLOCK

    def chunk(c):
        t0 = c * Q
        tpos = t0 + jnp.arange(Q)
        qc = lax.dynamic_slice_in_dim(qh, t0, Q, axis=3)
        gc = lax.dynamic_slice_in_dim(gh, t0, Q, axis=3)
        d_cmp = tpos[:, None] - cmp_end[None, :]
        b_cmp = rel_a[t5_bucket(d_cmp)].reshape(Q, n_cmp, G, R).transpose(2, 3, 0, 1)
        s_cmp = jnp.einsum('bgrqd,bgnd->bgrqn', qc, k_cmp) + b_cmp
        p_cmp = masked_softmax(s_cmp, d_cmp >= 0)
        o_cmp = jnp.einsum('bgrqn,bgnd->bgrqd', p_cmp.astype(v_cmp.dtype), v_cmp)
        imp = jnp.einsum('bgrqn,ns->bgqs', p_cmp, overlap)
        cur = tpos // SEL_BLOCK
        sb = jnp.arange(n_sb)[None, :]
        forced = (sb == 0) | (sb == cur[:, None]) | (sb == cur[:, None] - 1)
        imp = jnp.where(forced, TOP_BONUS, jnp.where(sb <= cur[:, None], imp, NEG_INF))
        _, idx = lax.top_k(imp, n_sel)
        k_sel = ks_blk[bi, gi, idx].reshape(b, G, Q, n_sel * SEL_BLOCK, dk)
        v_sel = vs_blk[bi, gi, idx].reshape(b, G, Q, n_sel * SEL_BLOCK, dk)
        kpos = (idx[..., None] * SEL_BLOCK + jnp.arange(SEL_BLOCK)).reshape(b, G, Q, n_sel * SEL_BLOCK)
        d_sel = tpos[None, None, :, None] - kpos
        b_sel = jnp.moveaxis(rel_g[t5_bucket(d_sel), gi], -1, 2)
        s_sel = jnp.einsum('bgrqd,bgqkd->bgrqk', qc, k_sel) + b_sel
        p_sel = masked_softmax(s_sel, (d_sel >= 0)[:, :, None])
        o_sel = jnp.einsum('bgrqk,bgqkd->bgrqd', p_sel.astype(v_sel.dtype), v_sel)
        k_w = lax.dynamic_slice_in_dim(kw_pad, t0, Q + WINDOW, axis=2)
        v_w = lax.dynamic_slice_in_dim(vw_pad, t0, Q + WINDOW, axis=2)
        wpos = t0 - WINDOW + jnp.arange(Q + WINDOW)
        d_w = tpos[:, None] - wpos[None, :]
        m_w = (d_w >= 0) & (d_w < WINDOW) & (wpos[None, :] >= 0)
        b_w = rel_a[t5_bucket(d_w)].reshape(Q, Q + WINDOW, G, R).transpose(2, 3, 0, 1)
        s_w = jnp.einsum('bgrqd,bgkd->bgrqk', qc, k_w) + b_w
        p_w = masked_softmax(s_w, m_w)
        o_w = jnp.einsum('bgrqk,bgkd->bgrqd', p_w.astype(v_w.dtype), v_w)
        return gc[..., 0:1] * o_cmp + gc[..., 1:2] * o_sel + gc[..., 2:3] * o_w

    out = lax.map(chunk, jnp.arange(s // Q))
    return out.transpose(1, 0, 4, 2, 3, 5).reshape(b, s, NSA_WIDTH)

def gla_mixer(q, k, v, log_a, r, norm_w):
    b, s, _ = q.shape
    H, DK, DV, C = GLA_HEADS, GLA_KEY_DIM, GLA_VAL_DIM, GLA_CHUNK
    n_c = s // C

    def to_chunks(t, d):
        return t.reshape(b, n_c, C, H, d).transpose(1, 0, 3, 2, 4).astype(jnp.float32)

    qc = to_chunks(q * DK ** -0.5, DK)
    kc = to_chunks(k, DK)
    vc = to_chunks(v, DV)
    gc = to_chunks(log_a, DK)
    causal = jnp.tril(jnp.ones((C, C), dtype=bool))[:, :, None]

    def step(state, inp):
        qi, ki, vi, gi = inp
        bcum = jnp.cumsum(gi, axis=2)
        o_inter = jnp.einsum('bhcd,bhde->bhce', qi * jnp.exp(bcum), state)
        diff = bcum[:, :, :, None, :] - bcum[:, :, None, :, :]
        decay = jnp.exp(jnp.where(causal, diff, NEG_INF))
        attn = jnp.einsum('bhid,bhjd,bhijd->bhij', qi, ki, decay)
        o_intra = jnp.einsum('bhij,bhje->bhie', attn, vi)
        b_last = bcum[:, :, -1:, :]
        new_state = state * jnp.exp(b_last[:, :, 0, :])[..., None] + jnp.einsum('bhcd,bhce->bhde', ki * jnp.exp(b_last - bcum), vi)
        return new_state, o_inter + o_intra

    state0 = jnp.zeros((b, H, DK, DV), jnp.float32)
    _, o = lax.scan(step, state0, (qc, kc, vc, gc))
    o = o.transpose(1, 0, 3, 2, 4).reshape(b, s, H, DV)
    o = rmsnorm(o, norm_w) * jax.nn.silu(r.reshape(b, s, H, DV).astype(jnp.float32))
    return o.reshape(b, s, H * DV).astype(r.dtype)

def moba_mixer(q, k, v, rel_c):
    b, s, _ = q.shape
    H, dh, Q = MOBA_HEADS, MOBA_HEAD_DIM, MOBA_Q_BLOCK
    qh = split_heads(q, H) * dh ** -0.5
    kh = split_heads(k, H)
    vh = split_heads(v, H)
    n_blk = -(-s // MOBA_BLOCK)
    pad = ((0, 0), (0, 0), (0, n_blk * MOBA_BLOCK - s), (0, 0))
    kp = jnp.pad(kh, pad)
    vp = jnp.pad(vh, pad)
    k_blk = kp.reshape(b, H, n_blk, MOBA_BLOCK, dh)
    v_blk = vp.reshape(b, H, n_blk, MOBA_BLOCK, dh)
    k_mean = jnp.mean(k_blk.astype(jnp.float32), axis=3)
    n_top = min(MOBA_TOPK, n_blk)
    ks_len = n_top * MOBA_BLOCK
    bi = jnp.arange(b)[:, None, None, None]
    hi = jnp.arange(H)[None, :, None, None]

    def chunk(c):
        t0 = c * Q
        tpos = t0 + jnp.arange(Q)
        qb = lax.dynamic_slice_in_dim(qh, t0, Q, axis=2)
        cur = t0 // MOBA_BLOCK
        score = jnp.einsum('bhqd,bhnd->bhqn', qb.astype(jnp.float32), k_mean)
        score = jnp.where(jnp.arange(n_blk) < cur, score, NEG_INF)
        _, idx = lax.top_k(score, n_top)
        sel_valid = idx < cur
        k_sel = k_blk[bi, hi, idx].reshape(b, H, Q, ks_len, dh)
        v_sel = v_blk[bi, hi, idx].reshape(b, H, Q, ks_len, dh)
        kpos = (idx[..., None] * MOBA_BLOCK + jnp.arange(MOBA_BLOCK)).reshape(b, H, Q, ks_len)
        s_sel = jnp.einsum('bhqd,bhqkd->bhqk', qb, k_sel) + rel_c[t5_bucket(tpos[None, None, :, None] - kpos), hi]
        m_sel = jnp.repeat(sel_valid, MOBA_BLOCK, axis=-1)
        k_own = lax.dynamic_slice_in_dim(kp, cur * MOBA_BLOCK, MOBA_BLOCK, axis=2)
        v_own = lax.dynamic_slice_in_dim(vp, cur * MOBA_BLOCK, MOBA_BLOCK, axis=2)
        d_own = tpos[:, None] - (cur * MOBA_BLOCK + jnp.arange(MOBA_BLOCK))[None, :]
        s_own = jnp.einsum('bhqd,bhkd->bhqk', qb, k_own) + rel_c[t5_bucket(d_own)].transpose(2, 0, 1)
        m_own = jnp.broadcast_to(d_own >= 0, (b, H, Q, MOBA_BLOCK))
        p = masked_softmax(jnp.concatenate([s_sel, s_own], axis=-1), jnp.concatenate([m_sel, m_own], axis=-1)).astype(v.dtype)
        return jnp.einsum('bhqk,bhqkd->bhqd', p[..., :ks_len], v_sel) + jnp.einsum('bhqk,bhkd->bhqd', p[..., ks_len:], v_own)

    out = lax.map(chunk, jnp.arange(s // Q))
    return out.transpose(1, 0, 3, 2, 4).reshape(b, s, MOBA_WIDTH)

def setup_inputs(seed: int = 0) -> dict:
    key = jax.random.key(seed)
    ks = jax.random.split(key, 22)
    L, dk = DEPTH, NSA_HEAD_DIM

    def nrm(k, shape, scale):
        return jax.random.normal(k, shape, jnp.float32) * scale

    return {
        'x': nrm(ks[0], (BATCH, SEQ, D_MODEL), 1.0),
        'rel_bias': nrm(ks[1], (NUM_BUCKETS, NSA_HEADS + MOBA_HEADS), 0.2),
        'norm_mix_pre': 1.0 + nrm(ks[2], (L, D_MODEL), 0.02),
        'norm_mix_post': 1.0 + nrm(ks[3], (L, D_MODEL), 0.02),
        'norm_ffn_pre': 1.0 + nrm(ks[4], (L, D_MODEL), 0.02),
        'norm_ffn_post': 1.0 + nrm(ks[5], (L, D_MODEL), 0.02),
        'w_in': nrm(ks[6], (L, D_MODEL, D_IN), D_MODEL ** -0.5),
        'nsa_pe_k': nrm(ks[7], (L, CMP_LEN, dk), 0.1),
        'nsa_pe_v': nrm(ks[8], (L, CMP_LEN, dk), 0.1),
        'nsa_cmp_k_w1': nrm(ks[9], (L, CMP_LEN * dk, dk), (CMP_LEN * dk) ** -0.5),
        'nsa_cmp_k_w2': nrm(ks[10], (L, dk, dk), dk ** -0.5),
        'nsa_cmp_v_w1': nrm(ks[11], (L, CMP_LEN * dk, dk), (CMP_LEN * dk) ** -0.5),
        'nsa_cmp_v_w2': nrm(ks[12], (L, dk, dk), dk ** -0.5),
        'gla_gate_w2': nrm(ks[13], (L, GLA_GATE_RANK, GLA_HEADS * GLA_KEY_DIM), GLA_GATE_RANK ** -0.5),
        'gla_gate_b': nrm(ks[14], (L, GLA_HEADS * GLA_KEY_DIM), 0.1),
        'gla_norm': 1.0 + nrm(ks[15], (L, GLA_VAL_DIM), 0.02),
        'w_branch_a': nrm(ks[16], (L, NSA_WIDTH, D_MODEL), NSA_WIDTH ** -0.5),
        'w_branch_b': nrm(ks[17], (L, GLA_HEADS * GLA_VAL_DIM, D_MODEL), (GLA_HEADS * GLA_VAL_DIM) ** -0.5),
        'w_branch_c': nrm(ks[18], (L, MOBA_WIDTH, D_MODEL), MOBA_WIDTH ** -0.5),
        'w_out': nrm(ks[19], (L, D_MODEL, D_MODEL), D_MODEL ** -0.5),
        'w_ffn_in': nrm(ks[20], (L, D_MODEL, 2 * FFN_HIDDEN), D_MODEL ** -0.5),
        'w_ffn_out': nrm(ks[21], (L, FFN_HIDDEN, D_MODEL), FFN_HIDDEN ** -0.5),
    }

def reference(x, rel_bias, norm_mix_pre, norm_mix_post, norm_ffn_pre, norm_ffn_post, w_in,
              nsa_pe_k, nsa_pe_v, nsa_cmp_k_w1, nsa_cmp_k_w2, nsa_cmp_v_w1, nsa_cmp_v_w2,
              gla_gate_w2, gla_gate_b, gla_norm, w_branch_a, w_branch_b, w_branch_c, w_out,
              w_ffn_in, w_ffn_out):
    b, s, _ = x.shape
    split_points = np.cumsum(SPLIT_SIZES)[:-1].tolist()
    rel_a = rel_bias[:, :NSA_HEADS]
    rel_c = rel_bias[:, NSA_HEADS:]
    for layer in range(DEPTH):
        h = rmsnorm(x, norm_mix_pre[layer])
        (a_q, a_kc, a_vc, a_ks, a_vs, a_kw, a_vw, a_g,
         b_q, b_k, b_v, b_r, b_lr, c_q, c_k, c_v, mg) = jnp.split(h @ w_in[layer], split_points, axis=-1)
        o_a = nsa_mixer(a_q, a_kc, a_vc, a_ks, a_vs, a_kw, a_vw, a_g, rel_a,
                        nsa_pe_k[layer], nsa_pe_v[layer], nsa_cmp_k_w1[layer], nsa_cmp_k_w2[layer],
                        nsa_cmp_v_w1[layer], nsa_cmp_v_w2[layer])
        log_a = jax.nn.log_sigmoid((b_lr @ gla_gate_w2[layer] + gla_gate_b[layer]).astype(jnp.float32)) / GLA_GATE_TAU
        o_b = gla_mixer(b_q, b_k, b_v, log_a, b_r, gla_norm[layer])
        o_c = moba_mixer(c_q, c_k, c_v, rel_c)
        g = jax.nn.sigmoid(mg).reshape(b, s, N_BRANCHES, D_MODEL)
        merged = (g[:, :, 0] * (o_a @ w_branch_a[layer])
                  + g[:, :, 1] * (o_b @ w_branch_b[layer])
                  + g[:, :, 2] * (o_c @ w_branch_c[layer]))
        x = x + rmsnorm(merged @ w_out[layer], norm_mix_post[layer])
        h = rmsnorm(x, norm_ffn_pre[layer])
        gate, up = jnp.split(h @ w_ffn_in[layer], 2, axis=-1)
        x = x + rmsnorm((jax.nn.silu(gate) * up) @ w_ffn_out[layer], norm_ffn_post[layer])
    return x


_drawn_inputs = setup_inputs


def setup_inputs(seed=0):
    import zlib

    import numpy as np

    out = dict(_drawn_inputs(seed))
    spreads = {}
    factors = {'norm_mix_post': 3.635,
     'norm_ffn_pre': 3.462,
     'norm_ffn_post': 16.234,
     'nsa_pe_k': 34.768,
     'gla_norm': 3.809,
     'rel_bias': 2.716,
     'nsa_pe_v': 4.48}
    for name, (base, spread) in spreads.items():
        noise = np.random.default_rng([zlib.crc32(name.encode()), seed]).standard_normal(out[name].shape)
        drawn = base * np.exp(spread * noise) if base else spread * noise
        out[name] = jnp.asarray(drawn.astype(out[name].dtype))
    for name, factor in factors.items():
        out[name] = (out[name] * factor).astype(out[name].dtype)
    return out
```

```python
from contextlib import ExitStack

import numpy as np

import concourse.bass as bass
from concourse import mybir

F32 = mybir.dt.float32
F32R = mybir.dt.float32r
BF16 = mybir.dt.bfloat16
U16 = mybir.dt.uint16
U8 = mybir.dt.uint8
ALU = mybir.AluOpType
ACT = mybir.ActivationFunctionType
AX = mybir.AxisListType

P = 128
SEQ, D = 512, 1024
NT = SEQ // P
KD = D // P
HID = 2816
NF = HID // P
EPS = 1e-6
MASKED = -1e30
CHUNK = 1024
RAW_SLOTS, SPLIT_SLOTS = 4, 2

A_Q, A_KC, A_VC, A_KS, A_VS, A_KW, A_VW, A_G = 0, 512, 640, 768, 896, 1024, 1152, 1280
B_Q, B_K, B_V, B_R, B_LR = 1304, 1560, 1816, 2328, 2840
C_Q, C_K, C_V, M_G = 2856, 3368, 3880, 4392

STRAIGHT = ([("ag", 0), ("blr", 0), ("bq", 0), ("bq", 1), ("bk", 0), ("bk", 1)]
            + [("bv", j) for j in range(4)] + [("br", j) for j in range(4)]
            + [("kc", 0), ("vc", 0), ("w1k", 0), ("w1k", 1), ("w1v", 0), ("w1v", 1), ("ks", 0), ("kw", 0)]
            + [("nv", 0), ("nv", 1)] + [("aq", j) for j in range(4)]
            + [("cq", j) for j in range(4)] + [("ck", j) for j in range(4)] + [("cv", j) for j in range(4)])
C_MERGE = len(STRAIGHT)
C_OUT = C_MERGE + 8 * 6
C_FIN = C_OUT + 8
C_FOUT = C_FIN + 2 * NF
N_CHUNKS = C_FOUT + NF
WIDTH = {"ag": KD * 24, "blr": KD * 16}
FIRST_MOBA = STRAIGHT.index(("cq", 0))
CMP_BACK = FIRST_MOBA + 3

S_GNORM, S_GB, S_W2, S_REL, S_PEK, S_PEV, S_CK2, S_CV2, S_END = 0, 1, 257, 513, 529, 561, 593, 657, 721
D0, D_TABLE = 544, 1056
GELU_1 = 2 * (2 / np.pi) ** 0.5
GELU_3 = GELU_1 * 0.044715
SBUF_BASE = 16512
LEVELS = [64, 32, 16, 8, 4, 2, 1]


def single_bank_chunks():
    index, n = {}, 0
    for c, (kind, j) in enumerate(STRAIGHT):
        if kind in ("bv", "br", "nv", "cv"):
            continue
        if kind in ("w1k", "w1v") and j == 1:
            index[c] = n - 1
            continue
        index[c] = n
        n += 1
    return index


SINGLE = single_bank_chunks()
TM_USE = {"bv": 0, "br": 1, "ot": 2, "nv": 3, "cv": 4}
AUX = (["lrT", "z0", "z1", "bT0", "bT1"] + [f"lv{l}_{t}" for l in range(8) for t in range(NT)]
       + ["kd0", "kd1", "o0", "s0", "o1", "s1", "o2", "s2", "o3", "cmp"])
AUX_AT = {name: i for i, name in enumerate(AUX)}
TILE_ORDER = (3, 0, 2, 1)
NSA_UNITS = [(br, 4 * g + p, i) for p in range(4) for g in range(2) for i in TILE_ORDER for br in ("s", "w")]
MOBA_UNITS = [("m", h, i) for h in range(8) for i in TILE_ORDER]
UNITS = NSA_UNITS + MOBA_UNITS
N_NSA = len(NSA_UNITS)
T_LAG, PV_LAG = 5, 7
STEPS = len(UNITS) + PV_LAG + 2


def program(nc, wpack, small_d, rows_d, onehot_d, mask_d, x_d, out_d):
    ctx = ExitStack()
    with ctx:
        def sem(name):
            return ctx.enter_context(nc.semaphore(name))

        bank = [ctx.enter_context(nc.psum_tensor(f"bank{i}", [P, 512], F32)) for i in range(8)]

        def at(kib, name, shape, dt=F32):
            return nc.alloc_sbuf_tensor_at(name, shape, dt, offset=int(SBUF_BASE + kib * 1024))

        hh = at(0, "h_hi", [P, KD, SEQ], F32R)
        hl = at(16, "h_lo", [P, KD, SEQ], F32R)
        raw = at(32, "w_raw", [P, RAW_SLOTS, CHUNK])
        wh = at(48, "w_hi", [P, SPLIT_SLOTS, CHUNK], F32R)
        wl = at(56, "w_lo", [P, SPLIT_SLOTS, CHUNK], F32R)
        small = at(64, "small", [P, S_END])
        ident = at(67, "ident", [P, P])
        tri = at(67.5, "tri", [P, P])
        lmask = at(106, "lmask", [P, 8, P], U16)
        gate = at(69, "gate", [P, NT, 24])
        stat = at(69.5, "stat", [P, 96])
        minus_half = at(69.875, "minus_half", [P, 4])
        gsq = at(70, "gsq", [P, 512])
        obh = at(72, "ob_hi", [P, 4, SEQ], F32R)
        obl = at(80, "ob_lo", [P, 4, SEQ], F32R)
        band = at(88, "band", [P, 16, 256])
        fullb = at(104, "fullb", [P, 2, 512])
        ghid = at(104, "ghid", [64, 6, P])
        cmpb = at(108, "cmpb", [P, NT, 8, 32])
        xs = at(112, "xs", [P, NT, D])
        onehot = at(128, "onehot", [97, D_TABLE], BF16)
        wpre = at(131, "wpre", [P, D])
        rel3 = at(136, "rel3", [97, 16], BF16)
        relb = at(136.25, "relb", [96, 3, 16], BF16)
        relr = at(136.5, "relr", [96, 2, 16])
        aqh = at(112, "aq_hi", [P, 4, SEQ], F32R)
        aql = at(120, "aq_lo", [P, 4, SEQ], F32R)
        akh = at(128, "ak_hi", [P, 2, SEQ], F32R)
        akl = at(132, "ak_lo", [P, 2, SEQ], F32R)
        av = at(136, "av", [P, NT, 256])
        kxh = at(140, "kx_hi", [P, 2, 32, 32], F32R)
        kxl = at(148, "kx_lo", [P, 2, 32, 32], F32R)
        gq = at(156, "gq", [P, 1024])
        gk = at(160, "gk", [P, 1024])
        gv = at(164, "gv", [P, NT, 512])
        gr = at(172, "gr", [P, NT, 512])
        gz = at(180, "gz", [P, 1024])
        zz = at(184, "zz", [P, 2, 1024])
        bT = at(192, "bT", [P, 1024])
        attnT = at(196, "attnT", [P, NT, 4, P])
        state = at(204, "state", [P, 2, 256])
        lr = at(206, "lr", [P, NT, 16])
        ebl = at(206.5, "ebl", [P, 8])
        pcs = at(188, "pcs", [P, NT * 8, 32])
        pcT = at(192, "pcT", [P, NT, 256])
        sc = at(164, "sc", [P, 8, 512])
        pT = [at(188, "pT0", [P, 512]), at(190, "pT1", [P, 512]), at(70, "pT2", [P, 512])]
        oah = at(112, "oa_hi", [P, 4, SEQ], F32R)
        oal = at(120, "oa_lo", [P, 4, SEQ], F32R)
        ckh = at(204, "ck_hi", [P, 32], F32R)
        ckl = at(204.125, "ck_lo", [P, 32], F32R)
        cvv = at(204.25, "cvv", [P, 2, 64])
        ast = at(204.75, "ast", [P, 8, 4])
        cst = at(205, "cst", [P, 4, 32])
        cqh = at(140, "cq_hi", [P, 4, SEQ], F32R)
        cql = at(148, "cq_lo", [P, 4, SEQ], F32R)
        kmh = at(180, "ckey_hi", [P, 4, SEQ], F32R)
        kml = at(196, "ckey_lo", [P, 4, SEQ], F32R)
        cv = at(156, "cv", [P, NT, 512])
        och = at(140, "oc_hi", [P, 4, SEQ], F32R)
        ocl = at(148, "oc_lo", [P, 4, SEQ], F32R)
        meh = at(156, "me_hi", [P, KD, SEQ], F32R)
        mel = at(172, "me_lo", [P, KD, SEQ], F32R)
        sig = at(188, "sig", [P, 2, SEQ])
        mrg = at(192, "mrg", [P, 2, SEQ])
        prod = at(196, "prod", [P, SEQ])
        xr = at(88, "xr", [P, NT, D])
        wpost = at(104, "wpost", [P, D])
        wfpre = at(108, "wfpre", [P, D])
        x1 = at(128, "x1", [P, NT, D])
        xn = at(144, "xn", [P, 2, D])
        junk = at(152, "junk", [P, 512])
        wfpost = at(160, "wfpost", [P, D])
        act = at(72, "act", [P, NF, SEQ])
        ash = at(116, "as_hi", [P, 2, SEQ], F32R)
        asl = at(120, "as_lo", [P, 2, SEQ], F32R)
        silu = at(124, "silu", [P, 2, SEQ])

        small_in, onehot_in, mask_in, wpre_in = sem("small_in"), sem("onehot_in"), sem("mask_in"), sem("wpre_in")
        x_in = [sem(f"x_in{t}") for t in range(NT)]
        xr_in, posts_in, wfpost_in, stored = sem("xr_in"), sem("posts_in"), sem("wfpost_in"), sem("stored")
        w_in = [sem(f"w_in{s}") for s in range(RAW_SLOTS)]
        w_hi = sem("w_hi")
        w_lo_pool, w_lo_dve = sem("w_lo_pool"), sem("w_lo_dve")
        w_used = sem("w_used")
        const_ready, zeros_ready = sem("const_ready"), sem("zeros_ready")
        dchain = sem("dchain")
        rel_ready, table_full, table_out = sem("rel_ready"), sem("table_full"), sem("table_out")
        sq_act, ms_ready, rstd_ready, xn_ready = sem("sq_act"), sem("ms_ready"), sem("rstd_ready"), sem("xn_ready")
        xT_full, h_hi, h_lo = sem("xT_full"), sem("h_hi"), sem("h_lo")
        s_free = [sem("s_free4"), sem("s_free5")]
        s_hi = sem("s_hi")
        tm_done, tm_exp = sem("tm_done"), sem("tm_exp")
        tm_free = [sem(f"tm_free{t}") for t in range(NT)]
        aux_done = sem("aux_done")
        aux_free = [sem("aux_free6"), sem("aux_free7")]
        gate_ready, pe_col = sem("gate_ready"), sem("pe_col")
        lr_ready, softplus, ls_ready = sem("lr_ready"), sem("softplus"), sem("ls_ready")
        e_ready, ex_ready, z_ready = sem("e_ready"), sem("ex_ready"), sem("z_ready")
        kd_ready, o_sq, o_ms, o_rstd = sem("kd_ready"), sem("o_sq"), sem("o_ms"), sem("o_rstd")
        state_ready, o_ready, ot_hi = sem("state_ready"), sem("o_ready"), sem("ot_hi")
        ot_full = sem("ot_full")
        hid_u, hid_e, hid_ready, cmp_ready = sem("hid_u"), sem("hid_e"), sem("hid_ready"), sem("cmp_ready")
        cs_full, cs_sub, cs_exp, cs_prob, cs_tr, cs_T = (sem("cs_full"), sem("cs_sub"), sem("cs_exp"),
                                                         sem("cs_prob"), sem("cs_tr"), sem("cs_T"))
        bias_ready, s_full, s_max, s_exp = sem("bias_ready"), sem("s_full"), sem("s_max"), sem("s_exp")
        s_rcp, s_prob, t_full, pv_done = sem("s_rcp"), sem("s_prob"), sem("t_full"), sem("pv_done")
        t_out = [sem("t_out_act"), sem("t_out_dve")]
        head_hi, head_lo = sem("head_hi"), sem("head_lo")
        d_sig, d_free, d_acc, d_mh, d_ml = sem("d_sig"), sem("d_free"), sem("d_acc"), sem("d_mh"), sem("d_ml")
        y_full, y_sq, y_ms, y_rstd, x1_ready = sem("y_full"), sem("y_sq"), sem("y_ms"), sem("y_rstd"), sem("x1_ready")
        x_sq, x_ms, x_rstd, n_ready, n_T = sem("x_sq"), sem("x_ms"), sem("x_rstd"), sem("n_ready"), sem("n_T")
        n_hi, n_lo = sem("n_hi"), sem("n_lo")
        f_sig, f_free, a_hi, a_lo = sem("f_sig"), sem("f_free"), sem("a_hi"), sem("a_lo")
        z_full, z_sq, z_ms, z_rstd, out_ready = (sem("z_full"), sem("z_sq"), sem("z_ms"), sem("z_rstd"),
                                                 sem("out_ready"))
        pe_rows = sem("pe_rows")
        block = ctx.enter_context(nc.Block())

        def landed(eng, slot, turn):
            eng.wait_ge(w_in[slot], 16 * (turn + 1))

        def lo_split(eng, c):
            if c < C_MERGE:
                eng.wait_ge(w_lo_pool, c + 1)
            else:
                eng.wait_ge(w_lo_dve, c + 1 - C_MERGE)

        def single_out(eng, c):
            eng.wait_ge(s_free[SINGLE[c] % 2], SINGLE[c] // 2 + 1)

        def tile_done(eng, c, group, t):
            if t < NT - 1:
                eng.wait_ge(tm_done, 3 * group + t + 1)
            else:
                eng.wait_ge(w_used, c + 1)

        def y_tile_done(eng, t):
            if t < NT - 1:
                eng.wait_ge(y_full, t + 1)
            else:
                eng.wait_ge(w_used, C_OUT + 8)

        def aux_full(eng, name):
            eng.wait_ge(aux_done, AUX_AT[name] + 1)

        def aux_out(eng, name):
            eng.wait_ge(aux_free[AUX_AT[name] % 2], AUX_AT[name] // 2 + 1)

        def aux_bank(name):
            return bank[6 + AUX_AT[name] % 2]

        def single_bank(c):
            return bank[4 + SINGLE[c] % 2]

        def slot_of(kind, j=0):
            return STRAIGHT.index((kind, j))

        def qkv(u):
            br, h, i = UNITS[u]
            if br == "m":
                b, p = 64 * (h % 2), h // 2
                return (cqh[b:b + 64, p], cql[b:b + 64, p], kmh[b:b + 64, p], kml[b:b + 64, p],
                        cv[:, :, 64 * h:64 * h + 64])
            g, p, s = h // 4, h % 4, 0 if br == "s" else 1
            b = 64 * g
            return (aqh[b:b + 64, p], aql[b:b + 64, p], akh[b:b + 64, s], akl[b:b + 64, s],
                    av[:, :, 128 * s + 64 * g:128 * s + 64 * g + 64])

        def head_of(u):
            if u < N_NSA:
                return u // 8, u % 8 == 0, u % 8 == 7
            return 8 + (u - N_NSA) // 4, u % 4 == 0, u % 4 == 3

        def score_bank(u):
            return bank[(0, 1, 6, 7)[u % 4]]

        def bias_head(n):
            return UNITS[8 * n][1] if n < 8 else n

        def output_bank(n):
            b = 64 * (n % 2)
            return bank[4 + n % 2][b:b + 64, :]

        def head_rows(n):
            hi_, lo_ = (oah, oal) if n < 8 else (och, ocl)
            b, p = 64 * (n % 2), n % 8 // 2
            return hi_[b:b + 64, p, :], lo_[b:b + 64, p, :]

        def level_view(ap, s):
            return ap.rearrange("p (n u s) -> p n u s", u=2, s=s)

        def transposed_hi(sa, t):
            for half in range(2):
                sa.wait_ge(n_T, 2 * t + half + 1)
                sa.activation(hh[:, 4 * half:4 * half + 4, P * t:P * t + P],
                              bank[4 * half + t][:, :].rearrange("p (k c) -> p k c", k=4),
                              ACT.Copy).then_inc(n_hi, 1)

        def attention_act(sa):
            for u in range(STEPS):
                if u < len(UNITS):
                    n = P * (UNITS[u][2] + 1)
                    sa.wait_ge(s_max, u + 1)
                    sa.activation(sc[:, u % 8, 0:n], sc[:, u % 8, 0:n], ACT.Exp, bias=ast[:, u % 8, 0:1],
                                  scale=-1.0, accum_out=ast[:, u % 8, 1:2]).then_inc(s_exp, 1)
                v = u - T_LAG
                if 0 <= v < len(UNITS) and v % 2 == 0:
                    n = P * (UNITS[v][2] + 1)
                    sa.wait_ge(t_full, v + 1)
                    if v >= 3:
                        sa.wait_ge(pv_done, v - 2)
                    sa.activation(pT[v % 3][:, 0:n], bank[2][:, 0:n], ACT.Copy).then_inc(t_out[0], 1)
                v = u - PV_LAG - 1
                if 0 <= v < len(UNITS) and head_of(v)[2]:
                    n = head_of(v)[0]
                    sa.wait_ge(pv_done, v + 1)
                    sa.activation(head_rows(n)[0], output_bank(n), ACT.Copy).then_inc(head_hi, 1)

        def transposed_lo(ve, t):
            for half in range(2):
                ve.wait_ge(n_hi, 2 * t + half + 1)
                ve.tensor_tensor(hl[:, 4 * half:4 * half + 4, P * t:P * t + P],
                                 bank[4 * half + t][:, :].rearrange("p (k c) -> p k c", k=4),
                                 hh[:, 4 * half:4 * half + 4, P * t:P * t + P].bitcast(F32),
                                 ALU.subtract).then_inc(n_lo, 1)

        def compressed_scores(ve, link):
            for t in range(NT):
                ve.wait_ge(cs_full, t // 2 + 1)
                ins = ve.tensor_tensor(pcs[:, 8 * t:8 * t + 8, :], bank[6 + t // 2][:, 256 * (t % 2):256 * (t % 2) + 256]
                                       .rearrange("p (h n) -> p h n", h=8), cmpb[:, t, :, :], ALU.add)
                link(ins)
            link(ve.tensor_reduce(cst[:, 0, :], pcs[:, :, :], AX.X, ALU.max))
            link(ve.tensor_scalar(cst[:, 0, :], cst[:, 0, :], -1e29, None, ALU.max))
            ve.tensor_tensor(pcs[:, :, :], pcs[:, :, :], cst[:, 0, :].unsqueeze(2).broadcast_to([P, 32, 32]),
                             ALU.subtract).then_inc(cs_sub, 1)
            ve.wait_ge(cs_exp, 1)
            link(ve.tensor_reduce(cst[:, 1, :], pcs[:, :, :], AX.X, ALU.add))
            link(ve.tensor_scalar(cst[:, 1, :], cst[:, 1, :], 1e-20, None, ALU.max))
            link(ve.reciprocal(cst[:, 2, :], cst[:, 1, :]))
            ve.wait_ge(gate_ready, 1)
            link(ve.tensor_tensor(cst[:, 3, :].rearrange("p (t h) -> p t h", t=NT),
                                  cst[:, 2, :].rearrange("p (t h) -> p t h", t=NT),
                                  gate[:, :, :].rearrange("p t (h b) -> p t h b", b=3)[:, :, :, 0], ALU.mult))
            ve.tensor_tensor(pcs[:, :, :], pcs[:, :, :], cst[:, 3, :].unsqueeze(2).broadcast_to([P, 32, 32]),
                             ALU.mult).then_inc(cs_prob, 1)

        def attention_dve(ve, link):
            def full_bias(n):
                h = bias_head(n)
                ve.tensor_copy(fullb[:, n % 2, 0:256], band[:, h, 0:1].broadcast_to([P, 256])).then_inc(bias_ready, 1)
                ve.tensor_copy(fullb[:, n % 2, 256:512], band[:, h, :]).then_inc(bias_ready, 1)

            full_bias(0)
            for u in range(STEPS):
                if u < len(UNITS):
                    n = P * (UNITS[u][2] + 1)
                    k, first, _ = head_of(u)
                    ve.wait_ge(s_full, u + 1)
                    if u >= 8:
                        ve.wait_ge(t_full, u - 7)
                    if first:
                        ve.wait_ge(bias_ready, 2 * k + 2)
                    ve.tensor_tensor_reduce(sc[:, u % 8, 0:n], score_bank(u)[:, 0:n], fullb[:, k % 2, 512 - n:512],
                                            -1.0, 3e38, ALU.add, ALU.min, ast[:, u % 8, 0:1]).then_inc(s_max, 1)
                    if first and k + 1 < 16:
                        if k > 0:
                            ve.wait_ge(s_max, u)
                        full_bias(k + 1)
                v = u - 1
                if 0 <= v < len(UNITS):
                    br, h, i = UNITS[v]
                    ve.wait_ge(s_exp, v + 1)
                    if br == "m":
                        ve.reciprocal(ast[:, v % 8, 2:3], ast[:, v % 8, 1:2]).then_inc(s_rcp, 1)
                    else:
                        g = 3 * h + (1 if br == "s" else 2)
                        link(ve.reciprocal(ast[:, v % 8, 3:4], ast[:, v % 8, 1:2]))
                        ve.tensor_tensor(ast[:, v % 8, 2:3], ast[:, v % 8, 3:4], gate[:, i, g:g + 1],
                                         ALU.mult).then_inc(s_rcp, 1)
                v = u - T_LAG
                if 0 <= v < len(UNITS) and v % 2 == 1:
                    n = P * (UNITS[v][2] + 1)
                    ve.wait_ge(t_full, v + 1)
                    if v >= 3:
                        ve.wait_ge(pv_done, v - 2)
                    ve.tensor_copy(pT[v % 3][:, 0:n], bank[3][:, 0:n]).then_inc(t_out[1], 1)
                    if v == len(UNITS) - 1:
                        ve.wait_ge(t_out[0], len(UNITS) // 2)
                        ve.engine_nop().then_inc(d_free, 2)
                v = u - PV_LAG - 2
                if 0 <= v < len(UNITS) and head_of(v)[2]:
                    n = head_of(v)[0]
                    hi_, lo_ = head_rows(n)
                    ve.wait_ge(head_hi, n + 1)
                    ve.tensor_tensor(lo_, output_bank(n), hi_.bitcast(F32), ALU.subtract).then_inc(head_lo, 1)

        def compressed_scores_pe(te, three, other_rows):
            te.wait_ge(cmp_ready, 8)
            single_out(te, slot_of("aq", 3))
            single_out(te, slot_of("aq", 2))
            for k in range(2):
                for h in range(8):
                    if h == 4:
                        other_rows(last)
                    for t in (2 * k, 2 * k + 1):
                        r = slice(64 * (h // 4), 64 * (h // 4) + 64)
                        cols = slice(t * P, t * P + P)
                        at_ = 256 * (t % 2) + 32 * h
                        last = three(bank[6 + k][:, at_:at_ + 32], aqh[r, h % 4, cols], aql[r, h % 4, cols],
                                     ckh[r, :], ckl[r, :], True, True)
                last.then_inc(cs_full, 1)

        def compressed_transposes(te):
            te.wait_ge(cs_prob, 1)
            for k in range(2):
                for t in range(2 * k, 2 * k + 2):
                    for g in range(2):
                        last = te.transpose(bank[6 + k][:, (2 * (t % 2) + g) * P:(2 * (t % 2) + g) * P + P],
                                            pcs[:, 8 * t + 4 * g:8 * t + 4 * g + 4, :].rearrange("p h n -> p (h n)"),
                                            ident[:, :])
                last.then_inc(cs_tr, 1)

        def attention_pe(te, mm, three):
            for t in range(NT):
                te.wait_ge(tm_free[t], 5)
            single_out(te, slot_of("ck", 3))
            single_out(te, slot_of("ck", 2))
            for u in range(STEPS):
                if u < len(UNITS):
                    br, h, i = UNITS[u]
                    qh, ql, kh, kl, _ = qkv(u)
                    n, cols = P * (i + 1), slice(P * i, P * i + P)
                    if u == 2:
                        te.wait_ge(cs_T, 2)
                    if u >= 4:
                        te.wait_ge(s_max, u - 3)
                    three(score_bank(u)[:, 0:n], qh[:, cols], ql[:, cols], kh[:, 0:n], kl[:, 0:n], True,
                          True).then_inc(s_full, 1)
                v = u - T_LAG
                if 0 <= v < len(UNITS):
                    te.wait_ge(s_prob, v + 1)
                    if v >= 2:
                        te.wait_ge(t_out[v % 2], v // 2)
                    for j in range(UNITS[v][2] + 1):
                        last = te.transpose(bank[2 + v % 2][:, P * j:P * j + P], sc[:, v % 8, P * j:P * j + P],
                                            ident[:, :])
                    last.then_inc(t_full, 1)
                v = u - PV_LAG
                if 0 <= v < len(UNITS):
                    br, h, i = UNITS[v]
                    values = qkv(v)[4]
                    n, first, _ = head_of(v)
                    if first and n >= 2:
                        te.wait_ge(head_lo, n - 1)
                    te.wait_ge(t_out[v % 2], v // 2 + 1)
                    out = output_bank(n)[:, P * i:P * i + P]
                    for j in range(i + 1):
                        last = mm(out, values[:, j, :], pT[v % 3][:, P * j:P * j + P], start=j == 0 and br != "w",
                                  stop=j == i and br == "m", skip_group_check=True)
                    if br == "w":
                        g, r = h // 4, 32 * (h % 4)
                        last = mm(out, cvv[r:r + 32, g, :], pcT[r:r + 32, i, g * P:g * P + P], start=False, stop=True,
                                  skip_group_check=True)
                    last.then_inc(pv_done, 1)

        @block.sync
        def _(sp):
            sp.dma_start(small[:, :], small_d[:, :]).then_inc(small_in, 16)
            for t in range(NT):
                sp.dma_start(xs[:, t, :], x_d[t * P:(t + 1) * P, :]).then_inc(x_in[t], 16)
            sp.dma_start(wpre[:, :], rows_d[0, :, :]).then_inc(wpre_in, 16)

            def fetch(c):
                if c >= RAW_SLOTS:
                    sp.wait_ge(w_hi, c - RAW_SLOTS + 1)
                    lo_split(sp, c - RAW_SLOTS)
                sp.dma_start(raw[:, c % RAW_SLOTS, :], wpack[c, :, :]).then_inc(w_in[c % RAW_SLOTS], 16)

            first = C_MERGE + 2 * RAW_SLOTS
            for c in range(first):
                fetch(c)
            sp.wait_ge(s_max, len(UNITS))
            sp.dma_start(xr[:, :, :], x_d.rearrange("(t p) d -> p t d", p=P)).then_inc(xr_in, 16)
            sp.dma_start(wpost[:, :], rows_d[1, :, :]).then_inc(posts_in, 16)
            sp.dma_start(wfpre[:, :], rows_d[2, :, :]).then_inc(posts_in, 16)
            with sp.Fori(0, (N_CHUNKS - first) // RAW_SLOTS) as i:
                for j in range(RAW_SLOTS):
                    c = first + j
                    sp.wait_ge(w_lo_dve, i * RAW_SLOTS + (c - RAW_SLOTS + 1 - C_MERGE))
                    sp.dma_start(raw[:, c % RAW_SLOTS, :],
                                 wpack[bass.ds(i * RAW_SLOTS + c, 1), :, :].rearrange("o p n -> (o p) n")
                                 ).then_inc(w_in[c % RAW_SLOTS], 16)
            for c in range(first + (N_CHUNKS - first) // RAW_SLOTS * RAW_SLOTS, N_CHUNKS):
                fetch(c)
            sp.dma_start(wfpost[:, :], rows_d[3, :, :]).then_inc(wfpost_in, 16)
            for t in range(NT):
                sp.wait_ge(out_ready, t + 1)
                sp.dma_start(out_d[0, t * P:(t + 1) * P, :], x1[:, t, :]).then_inc(stored, 16)
            sp.wait_ge(stored, 16 * NT)

        @block.gpsimd
        def _(pool):
            pool.memset(ident[:, :], 0.0).then_inc(zeros_ready, 1)
            pool.memset(tri[:, :], 1.0 / 16).then_inc(zeros_ready, 1)
            pool.memset(minus_half[:, :], -0.5).then_inc(zeros_ready, 1)
            pool.wait_ge(zeros_ready, 3)
            pool.affine_select(out=ident[:, :], in_=ident[:, :], compare_op=ALU.not_equal, fill=1.0, base=0,
                               pattern=[[-1, P]], channel_multiplier=1).then_inc(const_ready, 1)
            pool.affine_select(out=tri[:, :], in_=tri[:, :], compare_op=ALU.is_ge, fill=0.0, base=0,
                               pattern=[[1, P]], channel_multiplier=-1).then_inc(const_ready, 1)
            pool.memset(attnT[:, :, :, :], 0.0).then_inc(const_ready, 1)
            pool.wait_ge(ms_ready, 1)
            pool.tensor_tensor(stat[:, 4:8], stat[:, 0:4], minus_half[:, 0:4], ALU.pow).then_inc(rstd_ready, 1)

            def lo(c):
                s, b = c % RAW_SLOTS, c % SPLIT_SLOTS
                n = WIDTH.get(STRAIGHT[c][0], CHUNK)
                landed(pool, s, c // RAW_SLOTS)
                pool.wait_ge(w_hi, c + 1)
                pool.tensor_tensor(wl[:, b, 0:n], raw[:, s, 0:n], wh[:, b, 0:n].bitcast(F32),
                                   ALU.subtract).then_inc(w_lo_pool, 1)

            def scale(u):
                n = P * (UNITS[u][2] + 1)
                pool.wait_ge(s_rcp, u + 1)
                pool.wait_ge(s_exp, u + 1)
                pool.tensor_tensor(sc[:, u % 8, 0:n], sc[:, u % 8, 0:n],
                                   ast[:, u % 8, 2:3].broadcast_to([P, n]), ALU.mult).then_inc(s_prob, 1)

            lo(0)
            lo(1)
            for c in range(C_MERGE):
                if c + 2 < C_MERGE:
                    lo(c + 2)
                k = c - slot_of("w1k")
                if 0 <= k < NT:
                    pool.wait_ge(o_ms, k + 1)
                    pool.tensor_tensor(stat[:, 32 + 4 * k:36 + 4 * k], stat[:, 16 + 4 * k:20 + 4 * k],
                                       minus_half[:, 0:4], ALU.pow).then_inc(o_rstd, 1)
            for u in range(len(UNITS)):
                scale(u)
            for t in range(NT):
                pool.wait_ge(y_ms, t + 1)
                pool.tensor_tensor(stat[:, 8 + t:9 + t], stat[:, 4 + t:5 + t], minus_half[:, 0:1],
                                   ALU.pow).then_inc(y_rstd, 1)
                pool.wait_ge(x_ms, t + 1)
                pool.tensor_tensor(stat[:, 24 + t:25 + t], stat[:, 20 + t:21 + t], minus_half[:, 0:1],
                                   ALU.pow).then_inc(x_rstd, 1)
            for t in range(NT):
                pool.wait_ge(z_ms, t + 1)
                pool.tensor_tensor(stat[:, 40 + t:41 + t], stat[:, 36 + t:37 + t], minus_half[:, 0:1],
                                   ALU.pow).then_inc(z_rstd, 1)

        @block.scalar
        def _(sa):
            sa.dma_start(onehot[:, :].bitcast(U16), onehot_d[:, :]).then_inc(onehot_in, 16)
            sa.dma_start(lmask[:, :, :], mask_d[:, :, :]).then_inc(mask_in, 16)

            def hi(c):
                s, b = c % RAW_SLOTS, c % SPLIT_SLOTS
                n = WIDTH.get(STRAIGHT[c][0], CHUNK) if c < C_MERGE else CHUNK
                landed(sa, s, c // RAW_SLOTS)
                if c >= SPLIT_SLOTS:
                    sa.wait_ge(w_used, c - SPLIT_SLOTS + 1)
                sa.activation(wh[:, b, 0:n], raw[:, s, 0:n], ACT.Copy).then_inc(w_hi, 1)

            sa.wait_ge(small_in, 16)
            for i in range(10):
                sa.wait_ge(table_full, i + 1)
                ps = bank[i % 8]
                if i < 2:
                    for k in range(2):
                        ins = sa.activation(cmpb[:, 2 * i + k].rearrange("p h n -> p n h"),
                                            ps[:, 256 * k:256 * k + 256].rearrange("p (n h) -> p n h", h=8),
                                            ACT.Copy)
                else:
                    ins = sa.activation(band[:, :, 32 * (i - 2):32 * (i - 1)].rearrange("p h c -> p c h"),
                                        ps[:, :].rearrange("p (c h) -> p c h", h=16), ACT.Copy)
                ins.then_inc(table_out, 1)
                if i in (4, 6):
                    t = i // 2
                    sa.wait_ge(x_in[t], 16)
                    sa.activation(gr[:, 0:2, :].rearrange("p a b -> p (a b)"), xs[:, t, :], ACT.Square,
                                  accum_out=stat[:, 12 + t:13 + t]).then_inc(sq_act, 1)
                    sa.wait_ge(sq_act, t - 1)
            hi(0)
            hi(1)
            for k in range(KD):
                sa.wait_ge(xT_full, k + 1)
                sa.activation(hh[:, k, :], bank[k][:, :], ACT.Copy).then_inc(h_hi, 1)

            def prep_exp(l):
                sa.wait_ge(e_ready, 2 * l + 2)
                sa.activation(zz[:, l % 2, :], zz[:, l % 2, :], ACT.Exp).then_inc(ex_ready, 1)

            for c in range(C_MERGE):
                kind, j = STRAIGHT[c]
                hi(c + 2)
                ps = single_bank(c) if c in SINGLE else None
                done = s_free[SINGLE[c] % 2] if c in SINGLE else None
                if c in SINGLE:
                    sa.wait_ge(w_used, c + 1)
                if kind == "ag":
                    sa.activation(gate[:, :, :].rearrange("p t g -> p (t g)"), ps[:, 0:96], ACT.Exp,
                                  scale=-1.0).then_inc(done, 1)
                elif kind == "bq":
                    sa.activation(gq[:, 512 * j:512 * j + 512], ps[:, :], ACT.Copy, scale=0.125).then_inc(done, 1)
                elif kind == "bk":
                    sa.activation(gk[:, 512 * j:512 * j + 512], ps[:, :], ACT.Copy).then_inc(done, 1)
                elif kind in ("kc", "vc"):
                    kv = 0 if kind == "kc" else 1
                    sa.activation(kxh[:, kv, 0:16, 0:31],
                                  ps[:, 0:496].rearrange("p (n l) -> p l n", l=16), ACT.Copy).then_inc(s_hi, 1)
                    sa.activation(kxh[:, kv, 16:32, 0:31],
                                  ps[:, 16:512].rearrange("p (n l) -> p l n", l=16), ACT.Copy).then_inc(s_hi, 1)
                    sa.activation(kxh[:, kv, :, 31], small[:, (S_PEK, S_PEV)[kv]:(S_PEK, S_PEV)[kv] + 32],
                                  ACT.Copy).then_inc(pe_col, 1)
                elif kind in ("ks", "kw"):
                    sa.activation(akh[:, 0 if kind == "ks" else 1, :], ps[:, :], ACT.Copy).then_inc(s_hi, 1)
                elif kind in ("aq", "cq"):
                    sa.activation((aqh if kind == "aq" else cqh)[:, j, :], ps[:, :], ACT.Copy,
                                  scale=0.125).then_inc(s_hi, 1)
                elif kind == "ck":
                    sa.activation(kmh[:, j, :], ps[:, :], ACT.Copy).then_inc(s_hi, 1)
                elif kind == "bv" and j == 3:
                    for t in range(NT):
                        tile_done(sa, c, 0, t)
                        sa.activation(gv[:, t, :], bank[t][:, :], ACT.Copy).then_inc(tm_free[t], 1)
                elif kind == "br" and j == 3:
                    for t in range(NT):
                        tile_done(sa, c, 1, t)
                        sa.activation(gr[:, t, :], bank[t][:, :], ACT.Exp, scale=-1.0).then_inc(tm_exp, 1)
                elif kind == "nv" and j == 1:
                    for t in range(NT):
                        tile_done(sa, c, 2, t)
                        sa.activation(av[:, t, :], bank[t][:, 0:256], ACT.Copy).then_inc(tm_free[t], 1)
                elif kind == "cv" and j == 3:
                    for t in range(NT):
                        tile_done(sa, c, 3, t)
                        sa.activation(cv[:, t, :], bank[t][:, :], ACT.Copy).then_inc(tm_free[t], 1)
                if c == 3:
                    aux_out(sa, "z0")
                    aux_out(sa, "z1")
                    sa.activation(zz[:, 0, :], gz[:, :], ACT.Abs).then_inc(softplus, 1)
                    sa.wait_ge(softplus, 1)
                    sa.activation(zz[:, 0, :], zz[:, 0, :], ACT.Exp, scale=-1.0).then_inc(softplus, 1)
                    sa.wait_ge(softplus, 2)
                    sa.activation(zz[:, 0, :], zz[:, 0, :], ACT.Ln, bias=1.0).then_inc(softplus, 1)
                if c == 5:
                    for p in range(2):
                        aux_full(sa, f"bT{p}")
                        sa.activation(bT[:, 512 * p:512 * p + 512], aux_bank(f"bT{p}")[:, :],
                                      ACT.Copy).then_inc(aux_free[AUX_AT[f"bT{p}"] % 2], 1)
                if 6 <= c < 13:
                    prep_exp(c - 6)
                if c == 14:
                    sa.wait_ge(e_ready, 15)
                    sa.activation(zz[:, 0, :], zz[:, 0, :], ACT.Exp).then_inc(ex_ready, 1)
                    aux_full(sa, "lv5_3")
                    sa.activation(zz[:, 1, :], bT[:, :], ACT.Exp).then_inc(ex_ready, 1)
                    sa.activation(ebl[:, :], bT[:, :].rearrange("p (n c) -> p n c", c=P)[:, :, P - 1],
                                  ACT.Exp).then_inc(ex_ready, 1)
                if c == 15:
                    for k in range(2):
                        aux_full(sa, f"kd{k}")
                        sa.activation(gz[:, 512 * k:512 * k + 512], aux_bank(f"kd{k}")[:, :],
                                      ACT.Copy).then_inc(aux_free[AUX_AT[f"kd{k}"] % 2], 1)
                if 16 <= c < 20:
                    t = c - 16
                    aux_full(sa, f"o{t}")
                    if t > 0:
                        sa.wait_ge(o_ms, t)
                    sa.activation(gsq[:, :], aux_bank(f"o{t}")[:, :], ACT.Square).then_inc(o_sq, 1)
                if c == 20:
                    for t in range(NT):
                        sa.wait_ge(ot_full, t + 1)
                        sa.activation(obh[:, :, P * t:P * t + P], bank[t][:, :].rearrange("p (h c) -> p h c", h=4),
                                      ACT.Copy, scale=small[:, S_GNORM:S_GNORM + 1]).then_inc(ot_hi, 1)
                    sa.wait_ge(hid_u, 1)
                    sa.activation(ghid[:, 3, :], ghid[:, 2, :], ACT.Exp, scale=-1.0).then_inc(hid_e, 1)
                if c == FIRST_MOBA - 1:
                    sa.wait_ge(cs_sub, 1)
                    sa.activation(pcs[:, :, :], pcs[:, :, :], ACT.Exp).then_inc(cs_exp, 1)
                if c == CMP_BACK:
                    for k in range(2):
                        sa.wait_ge(cs_tr, k + 1)
                        sa.activation(pcT[:, 2 * k:2 * k + 2, :].rearrange("p a b -> p (a b)"), bank[6 + k][:, :],
                                      ACT.Copy).then_inc(cs_T, 1)
            attention_act(sa)

            with sa.Fori(0, 4) as i:
                for s in range(6):
                    for part in range(2):
                        c = C_MERGE + 2 * s + 2 + part
                        n = CHUNK if part == 0 or s == 5 else CHUNK // 2
                        if part == 1:
                            sa.wait_ge(w_used, i * 12 + C_MERGE + 2 * s + 1)
                            sa.wait_ge(d_free, i * 6 + s + 1)
                            sa.activation(sig[:, s % 2, :], bank[s % 2][:, :], ACT.Sigmoid).then_inc(d_sig, 1)
                        sa.wait_ge(w_in[c % RAW_SLOTS], i * 48 + 16 * (c // RAW_SLOTS + 1))
                        sa.wait_ge(w_used, i * 12 + c - SPLIT_SLOTS + 1)
                        sa.activation(wh[:, c % 2, 0:n], raw[:, c % RAW_SLOTS, 0:n], ACT.Copy).then_inc(w_hi, 1)
                    if s % 3 == 2:
                        sa.wait_ge(d_acc, i * 4 + 2 * (s // 3) + 2)
                        sa.activation(meh[:, bass.ds(i * 2 + s // 3, 1), :].rearrange("p o n -> p (o n)"),
                                      mrg[:, s // 3, :], ACT.Copy).then_inc(d_mh, 1)
            for m in range(7):
                hi(C_OUT + m + 2)
            for t in range(NT):
                y_tile_done(sa, t)
                for half in range(2):
                    if 2 * t + half + t > 0:
                        sa.wait_ge(y_sq, 2 * t + half)
                    sa.activation(junk[:, :], bank[4 * (1 - half) + t][:, :], ACT.Square,
                                  accum_out=stat[:, 48 + 2 * t + half:49 + 2 * t + half]).then_inc(y_sq, 1)
                sa.wait_ge(x1_ready, t + 1)
                sa.activation(xn[:, t % 2, :], x1[:, t, :], ACT.Square,
                              accum_out=stat[:, 28 + t:29 + t]).then_inc(x_sq, 1)
                if t > 0:
                    transposed_hi(sa, t - 1)
                else:
                    hi(C_OUT + 9)
            transposed_hi(sa, NT - 1)
            with sa.Fori(0, NF // 2) as i:
                for f in range(2):
                    for part in range(2):
                        c = C_FIN + 2 * f + 2 + part
                        if part == 1:
                            sa.wait_ge(w_used, i * 4 + C_FIN + 2 * f + 1)
                            sa.wait_ge(f_free, i * 2 + f + 1)
                            sa.activation(silu[:, f, :], bank[2 * f][:, :], ACT.Silu).then_inc(f_sig, 1)
                        sa.wait_ge(w_in[c % RAW_SLOTS], i * 16 + 16 * (c // RAW_SLOTS + 1))
                        sa.wait_ge(w_used, i * 4 + c - SPLIT_SLOTS + 1)
                        sa.activation(wh[:, c % 2, :], raw[:, c % RAW_SLOTS, :], ACT.Copy).then_inc(w_hi, 1)

            def act_hi(k):
                sa.wait_ge(f_free, k + 3)
                if k >= 2:
                    sa.wait_ge(w_used, C_FOUT + k - 1)
                sa.activation(ash[:, k % 2, :], act[:, k, :], ACT.Copy).then_inc(a_hi, 1)

            for k in range(4):
                act_hi(k)
                if k >= 2:
                    hi(C_FOUT + k)
            with sa.Fori(0, 4) as i:
                for k in range(4, 8):
                    c = C_FOUT + k
                    sa.wait_ge(w_used, i * 4 + c - 1)
                    sa.activation(ash[:, k % 2, :], act[:, bass.ds(i * 4 + k, 1), :].rearrange("p o n -> p (o n)"),
                                  ACT.Copy).then_inc(a_hi, 1)
                    sa.wait_ge(w_in[c % RAW_SLOTS], i * 16 + 16 * (c // RAW_SLOTS + 1))
                    sa.activation(wh[:, c % 2, :], raw[:, c % RAW_SLOTS, :], ACT.Copy).then_inc(w_hi, 1)
            for k in range(20, NF):
                act_hi(k)
                hi(C_FOUT + k)
            for t in range(NT):
                sa.wait_ge(z_full, t + 1)
                for half in range(2):
                    if t + half > 0:
                        sa.wait_ge(z_sq, 2 * t + half)
                    sa.activation(junk[:, :], bank[4 * half + t][:, :], ACT.Square,
                                  accum_out=stat[:, 56 + 2 * t + half:57 + 2 * t + half]).then_inc(z_sq, 1)

        @block.vector
        def _(ve):
            chain = [0]

            def link(ins):
                chain[0] += 1
                ins.then_inc(dchain, 1)
                ve.wait_ge(dchain, chain[0])

            ve.wait_ge(small_in, 16)
            rel = small[0:96, S_REL:S_REL + 16]
            link(ve.tensor_copy(relb[:, 0, :], rel))
            link(ve.tensor_tensor(relr[:, 0, :], rel, relb[:, 0, :], ALU.subtract))
            link(ve.tensor_copy(relb[:, 1, :], relr[:, 0, :]))
            link(ve.tensor_tensor(relr[:, 1, :], relr[:, 0, :], relb[:, 1, :], ALU.subtract))
            link(ve.tensor_copy(relb[:, 2, :], relr[:, 1, :]))
            for k in range(3):
                ve.tensor_copy(rel3[32 * k:32 * k + 32, :], relb[32 * k:32 * k + 32, k, :]).then_inc(rel_ready, 1)
            ve.memset(rel3[96:97, :], MASKED).then_inc(rel_ready, 1)
            for t in range(2):
                ve.wait_ge(x_in[t], 16)
                link(ve.tensor_tensor_reduce(gv[:, 2 * t:2 * t + 2, :].rearrange("p a b -> p (a b)"), xs[:, t, :],
                                             xs[:, t, :], 1.0, 0.0, ALU.mult, ALU.add, stat[:, 12 + t:13 + t]))
            ve.wait_ge(sq_act, 2)
            ve.tensor_scalar(stat[:, 0:4], stat[:, 12:16], 1.0 / D, EPS, ALU.mult, ALU.add).then_inc(ms_ready, 1)
            ve.wait_ge(rstd_ready, 1)
            ve.wait_ge(wpre_in, 16)
            for t in range(NT):
                ve.scalar_tensor_tensor(out=xs[:, t, :], in0=xs[:, t, :], scalar=stat[:, 4 + t:5 + t],
                                        in1=wpre[:, :], op0=ALU.mult, op1=ALU.mult).then_inc(xn_ready, 1)
            for k in range(KD):
                ve.wait_ge(h_hi, k + 1)
                ve.tensor_tensor(hl[:, k, :], bank[k][:, :], hh[:, k, :].bitcast(F32),
                                 ALU.subtract).then_inc(h_lo, 1)

            def lo(c):
                b = c % SPLIT_SLOTS
                ve.wait_ge(w_hi, c + 1)
                ve.tensor_tensor(wl[:, b, :], raw[:, c % RAW_SLOTS, :], wh[:, b, :].bitcast(F32),
                                 ALU.subtract).then_inc(w_lo_dve, 1)

            def gla_sub(l):
                s = LEVELS[l]
                z, b = level_view(zz[:, l % 2, :], s), level_view(bT[:, :], s)
                n = 512 // s
                if l == 0:
                    ve.wait_ge(ls_ready, 1)
                    aux_out(ve, "bT1")
                    aux_out(ve, "bT0")
                if l >= 2:
                    aux_full(ve, f"lv{l - 2}_3")
                ref = b[:, :, 0, s - 1:s].broadcast_to([P, n, s])
                ve.tensor_tensor(z[:, :, 0, :], ref, b[:, :, 0, :], ALU.subtract).then_inc(e_ready, 1)
                ve.tensor_tensor(z[:, :, 1, :], b[:, :, 1, :], ref, ALU.subtract).then_inc(e_ready, 1)

            def gla_mul(l):
                s = LEVELS[l]
                z = level_view(zz[:, l % 2, :], s)
                ve.wait_ge(ex_ready, l + 1)
                if l == 0:
                    single_out(ve, slot_of("bq", 1))
                    single_out(ve, slot_of("bk", 0))
                    single_out(ve, slot_of("bk", 1))
                ve.tensor_tensor(z[:, :, 0, :], z[:, :, 0, :], level_view(gk[:, :], s)[:, :, 0, :],
                                 ALU.mult).then_inc(z_ready, 1)
                ve.tensor_tensor(z[:, :, 1, :], z[:, :, 1, :], level_view(gq[:, :], s)[:, :, 1, :],
                                 ALU.mult).then_inc(z_ready, 1)

            def gla_pick(l):
                for t in range(NT):
                    aux_full(ve, f"lv{l}_{t}")
                    if l == 0 and t == 0:
                        ve.wait_ge(mask_in, 16)
                        ve.wait_ge(const_ready, 3)
                    if l > 0:
                        aux_out(ve, f"lv{l - 1}_{t}")
                    ve.copy_predicated(attnT[:, t, :, :], lmask[:, l:l + 1, :].broadcast_to([P, 4, P]),
                                       aux_bank(f"lv{l}_{t}")[:, :].rearrange("p (h c) -> p h c", h=4)
                                       ).then_inc(aux_free[AUX_AT[f"lv{l}_{t}"] % 2], 1)

            def silu_r(t):
                ve.wait_ge(tm_exp, t + 1)
                link(ve.tensor_scalar(gr[:, t, :], gr[:, t, :], 1.0, None, ALU.add))
                link(ve.reciprocal(gr[:, t, :], gr[:, t, :]))
                ve.tensor_tensor(gr[:, t, :], gr[:, t, :], bank[t][:, :], ALU.mult).then_inc(tm_free[t], 1)

            for c in range(C_MERGE):
                kind, j = STRAIGHT[c]
                ps = single_bank(c) if c in SINGLE else None
                done = s_free[SINGLE[c] % 2] if c in SINGLE else None
                if kind == "ag":
                    single_out(ve, c)
                    g2 = gate[:, :, :].rearrange("p t g -> p (t g)")
                    link(ve.tensor_scalar(g2, g2, 1.0, None, ALU.add))
                    ve.reciprocal(g2, g2).then_inc(gate_ready, 1)
                elif kind == "blr":
                    ve.wait_ge(w_used, c + 1)
                    ve.tensor_copy(lr[:, :, :], ps[:, 0:64].rearrange("p (t r) -> p t r", t=NT)).then_inc(done, 1)
                elif kind in ("kc", "vc"):
                    kv = 0 if kind == "kc" else 1
                    ve.wait_ge(w_used, c + 1)
                    ve.wait_ge(pe_col, kv + 1)
                    pe0 = (S_PEK, S_PEV)[kv]
                    link(ve.tensor_tensor(kxl[:, kv, :, 31], small[:, pe0:pe0 + 32],
                                          kxh[:, kv, :, 31].bitcast(F32), ALU.subtract))
                    ve.wait_ge(s_hi, 2 * kv + 2)
                    link(ve.tensor_tensor(kxl[:, kv, 0:16, 0:31], ps[:, 0:496].rearrange("p (n l) -> p l n", l=16),
                                          kxh[:, kv, 0:16, 0:31].bitcast(F32), ALU.subtract))
                    ve.tensor_tensor(kxl[:, kv, 16:32, 0:31], ps[:, 16:512].rearrange("p (n l) -> p l n", l=16),
                                     kxh[:, kv, 16:32, 0:31].bitcast(F32), ALU.subtract).then_inc(done, 1)
                elif kind in ("w1k", "w1v") and j == 1:
                    kv = 0 if kind == "w1k" else 1
                    ve.wait_ge(w_used, c + 1)
                    hidden = ps[0:64, 0:64].rearrange("p (g n) -> p g n", g=2)
                    link(ve.tensor_copy(ghid[:, 4, 64 * kv:64 * kv + 2], hidden[:, :, 31]))
                    ve.tensor_tensor(ghid[:, 0, 64 * kv:64 * kv + 64].rearrange("p (g n) -> p g n", g=2), hidden,
                                     ghid[:, 4, 64 * kv:64 * kv + 2].unsqueeze(2).broadcast_to([64, 2, 32]),
                                     ALU.add).then_inc(done, 1)
                elif kind in ("ks", "kw", "aq", "cq", "ck"):
                    order = [x for x in STRAIGHT if x[0] in ("ks", "kw", "aq", "cq", "ck")]
                    ve.wait_ge(s_hi, 4 + order.index((kind, j)) + 1)
                    h_, l_ = {"ks": (akh, akl), "kw": (akh, akl), "aq": (aqh, aql), "cq": (cqh, cql),
                              "ck": (kmh, kml)}[kind]
                    k = {"ks": 0, "kw": 1}.get(kind, j)
                    ve.scalar_tensor_tensor(out=l_[:, k, :], in0=ps[:, :],
                                            scalar=0.125 if kind in ("aq", "cq") else 1.0,
                                            in1=h_[:, k, :].bitcast(F32), op0=ALU.mult,
                                            op1=ALU.subtract).then_inc(done, 1)
                if c == 2:
                    aux_full(ve, "lrT")
                    ve.tensor_copy(gsq[0:16, :], aux_bank("lrT")[0:16, :]).then_inc(aux_free[0], 1)
                if c == 3:
                    for k in range(2):
                        aux_full(ve, f"z{k}")
                        ve.tensor_tensor(gz[:, 512 * k:512 * k + 512].rearrange("p (t n) -> p t n", t=2),
                                         aux_bank(f"z{k}")[:, :].rearrange("p (t n) -> p t n", t=2),
                                         small[:, S_GB:S_GB + 256].unsqueeze(1).broadcast_to([P, 2, 256]),
                                         ALU.add).then_inc(aux_free[AUX_AT[f"z{k}"] % 2], 1)
                    ve.wait_ge(softplus, 3)
                    aux_out(ve, "z0")
                    aux_out(ve, "z1")
                    ve.scalar_tensor_tensor(out=gz[:, :], in0=gz[:, :], scalar=0.0, in1=zz[:, 0, :], op0=ALU.min,
                                            op1=ALU.subtract).then_inc(ls_ready, 1)
                if 6 <= c < 13:
                    gla_sub(c - 6)
                    if c > 6:
                        gla_pick(c - 7)
                    gla_mul(c - 6)
                if c == 13:
                    gla_pick(6)
                if c == 14:
                    b3 = bT[:, :].rearrange("p (n c) -> p n c", c=P)
                    ve.tensor_tensor(zz[:, 0, :].rearrange("p (n c) -> p n c", c=P),
                                     b3[:, :, P - 1:P].broadcast_to([P, 8, P]), b3, ALU.subtract).then_inc(e_ready, 1)
                    gla_pick(7)
                    ve.wait_ge(ex_ready, 10)
                    ve.tensor_tensor(zz[:, 0, :], zz[:, 0, :], gk[:, :], ALU.mult).then_inc(kd_ready, 1)
                    ve.tensor_tensor(zz[:, 1, :], zz[:, 1, :], gq[:, :], ALU.mult).then_inc(kd_ready, 1)
                if 13 <= c < 17:
                    silu_r(c - 13)
                if 16 <= c < 20:
                    t = c - 16
                    if t < 3:
                        aux_full(ve, f"s{t}")
                        ps_s = aux_bank(f"s{t}")[:, :].rearrange("p (a n) -> p a n", a=2)
                        if t == 0:
                            ve.tensor_copy(state[:, :, :], ps_s).then_inc(aux_free[AUX_AT["s0"] % 2], 1)
                        else:
                            aux_out(ve, f"s{t - 1}")
                            link(ve.scalar_tensor_tensor(out=state[:, 0, :], in0=state[:, 0, :],
                                                         scalar=ebl[:, t:t + 1], in1=ps_s[:, 0, :],
                                                         op0=ALU.mult, op1=ALU.add))
                            ve.scalar_tensor_tensor(out=state[:, 1, :], in0=state[:, 1, :],
                                                    scalar=ebl[:, 4 + t:5 + t], in1=ps_s[:, 1, :],
                                                    op0=ALU.mult, op1=ALU.add
                                                    ).then_inc(aux_free[AUX_AT[f"s{t}"] % 2], 1)
                    ve.wait_ge(o_sq, t + 1)
                    link(ve.tensor_reduce(stat[:, 64 + 4 * t:68 + 4 * t],
                                          gsq[:, :].rearrange("p (h c) -> p h c", h=4), AX.X, ALU.add))
                    ve.tensor_scalar(stat[:, 16 + 4 * t:20 + 4 * t], stat[:, 64 + 4 * t:68 + 4 * t], 1.0 / 128, EPS,
                                     ALU.mult, ALU.add).then_inc(o_ms, 1)
                    ve.wait_ge(o_rstd, t + 1)
                    ve.wait_ge(tm_free[t], 2)
                    ps_o = aux_bank(f"o{t}")
                    for h in range(4):
                        ins = ve.scalar_tensor_tensor(out=gr[:, t, P * h:P * h + P], in0=ps_o[:, P * h:P * h + P],
                                                      scalar=stat[:, 32 + 4 * t + h:33 + 4 * t + h],
                                                      in1=gr[:, t, P * h:P * h + P], op0=ALU.mult, op1=ALU.mult)
                    ins.then_inc(aux_free[AUX_AT[f"o{t}"] % 2], 1)
                if c == 20:
                    for t in range(NT):
                        ve.wait_ge(ot_hi, t + 1)
                        ve.scalar_tensor_tensor(out=obl[:, :, P * t:P * t + P],
                                                in0=bank[t][:, :].rearrange("p (h c) -> p h c", h=4),
                                                scalar=small[:, S_GNORM:S_GNORM + 1],
                                                in1=obh[:, :, P * t:P * t + P].bitcast(F32), op0=ALU.mult,
                                                op1=ALU.subtract).then_inc(tm_free[t], 1)
                    single_out(ve, slot_of("w1k", 1))
                    single_out(ve, slot_of("w1v", 1))
                    link(ve.tensor_tensor(ghid[:, 1, :], ghid[:, 0, :], ghid[:, 0, :], ALU.mult))
                    link(ve.tensor_scalar(ghid[:, 1, :], ghid[:, 1, :], GELU_3, GELU_1, ALU.mult, ALU.add))
                    link(ve.tensor_tensor(ghid[:, 2, :], ghid[:, 1, :], ghid[:, 0, :], ALU.mult))
                    ve.tensor_scalar(ghid[:, 2, :], ghid[:, 2, :], -80.0, None, ALU.max).then_inc(hid_u, 1)
                    ve.wait_ge(hid_e, 1)
                    link(ve.tensor_scalar(ghid[:, 3, :], ghid[:, 3, :], 1.0, None, ALU.add))
                    link(ve.reciprocal(ghid[:, 3, :], ghid[:, 3, :]))
                    ve.tensor_tensor(ghid[:, 5, :], ghid[:, 3, :], ghid[:, 0, :], ALU.mult).then_inc(hid_ready, 1)
                if c == 21:
                    aux_full(ve, "cmp")
                    ps_c = aux_bank("cmp")
                    for g in range(2):
                        link(ve.tensor_copy(ckh[64 * g:64 * g + 64, :], ps_c[0:64, 32 * g:32 * g + 32]))
                        link(ve.tensor_tensor(ckl[64 * g:64 * g + 64, :], ps_c[0:64, 32 * g:32 * g + 32],
                                              ckh[64 * g:64 * g + 64, :].bitcast(F32), ALU.subtract))
                        for r in range(4):
                            ins = ve.tensor_copy(cvv[32 * r:32 * r + 32, g, :], ps_c[32 * g:32 * g + 32, 64:128])
                            ins.then_inc(cmp_ready, 1)
                if c == FIRST_MOBA - 1:
                    compressed_scores(ve, link)
                if c + 2 >= C_MERGE:
                    lo(c + 2)

            attention_dve(ve, link)
            with ve.Fori(0, 4) as i:
                for s in range(6):
                    for part in range(2):
                        c = C_MERGE + 2 * s + 2 + part
                        n = CHUNK if part == 0 or s == 5 else CHUNK // 2
                        ve.wait_ge(w_hi, i * 12 + c + 1)
                        ve.tensor_tensor(wl[:, c % 2, 0:n], raw[:, c % RAW_SLOTS, 0:n],
                                         wh[:, c % 2, 0:n].bitcast(F32), ALU.subtract).then_inc(w_lo_dve, 1)
                        if part == 0:
                            ve.wait_ge(d_sig, i * 6 + s + 1)
                            ve.wait_ge(w_used, i * 12 + C_MERGE + 2 * s + 2)
                            m, b = mrg[:, s // 3, :], s % 3
                            ve.tensor_tensor(m if b == 0 else prod[:, :], sig[:, s % 2, :], bank[2 + s % 2][:, :],
                                             ALU.mult).then_inc(d_free, 1)
                            if b > 0:
                                ve.wait_ge(d_free, i * 6 + s + 3)
                                if b == 2:
                                    ve.wait_ge(d_acc, i * 4 + 2 * (s // 3) + 1)
                                ve.tensor_tensor(m, m, prod[:, :], ALU.add).then_inc(d_acc, 1)
                    if s % 3 == 2:
                        ve.wait_ge(d_mh, i * 2 + s // 3 + 1)
                        me_n = bass.ds(i * 2 + s // 3, 1)
                        ve.tensor_tensor(mel[:, me_n, :].rearrange("p o n -> p (o n)"), mrg[:, s // 3, :],
                                         meh[:, me_n, :].rearrange("p o n -> p (o n)").bitcast(F32),
                                         ALU.subtract).then_inc(d_ml, 1)

            for m in range(7):
                lo(C_OUT + m + 2)

            def y_mean(t):
                ve.wait_ge(y_sq, 2 * t + 2)
                link(ve.tensor_tensor(stat[:, t:t + 1], stat[:, 48 + 2 * t:49 + 2 * t],
                                      stat[:, 49 + 2 * t:50 + 2 * t], ALU.add))
                ve.tensor_scalar(stat[:, 4 + t:5 + t], stat[:, t:t + 1], 1.0 / D, EPS, ALU.mult,
                                 ALU.add).then_inc(y_ms, 1)

            ve.wait_ge(xr_in, 16)
            ve.wait_ge(posts_in, 32)
            y_mean(0)
            for t in range(NT):
                ve.wait_ge(y_rstd, t + 1)
                for half in range(2):
                    link(ve.scalar_tensor_tensor(out=x1[:, t, 512 * half:512 * half + 512],
                                                 in0=bank[4 * (1 - half) + t][:, :], scalar=stat[:, 8 + t:9 + t],
                                                 in1=wpost[:, 512 * half:512 * half + 512], op0=ALU.mult,
                                                 op1=ALU.mult))
                ve.tensor_tensor(x1[:, t, :], x1[:, t, :], xr[:, t, :], ALU.add).then_inc(x1_ready, 1)
                if t + 1 < NT:
                    y_mean(t + 1)
                ve.wait_ge(x_sq, t + 1)
                ve.tensor_scalar(stat[:, 20 + t:21 + t], stat[:, 28 + t:29 + t], 1.0 / D, EPS, ALU.mult,
                                 ALU.add).then_inc(x_ms, 1)
                if t > 0:
                    transposed_lo(ve, t - 1)
                else:
                    lo(C_OUT + 9)
                ve.wait_ge(x_rstd, t + 1)
                ve.wait_ge(x1_ready, t + 1)
                ve.scalar_tensor_tensor(out=xn[:, t % 2, :], in0=x1[:, t, :], scalar=stat[:, 24 + t:25 + t],
                                        in1=wfpre[:, :], op0=ALU.mult, op1=ALU.mult).then_inc(n_ready, 1)
            transposed_lo(ve, NT - 1)
            ve.engine_nop().then_inc(f_free, 2)
            with ve.Fori(0, NF // 2) as i:
                for f in range(2):
                    for part in range(2):
                        c = C_FIN + 2 * f + 2 + part
                        ve.wait_ge(w_hi, i * 4 + c + 1)
                        ve.tensor_tensor(wl[:, c % 2, :], raw[:, c % RAW_SLOTS, :], wh[:, c % 2, :].bitcast(F32),
                                         ALU.subtract).then_inc(w_lo_dve, 1)
                        if part == 0:
                            ve.wait_ge(f_sig, i * 2 + f + 1)
                            ve.wait_ge(w_used, i * 4 + C_FIN + 2 * f + 2)
                            ve.tensor_tensor(act[:, bass.ds(i * 2 + f, 1), :].rearrange("p o n -> p (o n)"),
                                             silu[:, f, :], bank[2 * f + 1][:, :], ALU.mult).then_inc(f_free, 1)

            def act_lo(k):
                ve.wait_ge(a_hi, k + 1)
                ve.tensor_tensor(asl[:, k % 2, :], act[:, k, :], ash[:, k % 2, :].bitcast(F32),
                                 ALU.subtract).then_inc(a_lo, 1)

            for k in range(4):
                act_lo(k)
                if k >= 2:
                    lo(C_FOUT + k)
            with ve.Fori(0, 4) as i:
                for k in range(4, 8):
                    c = C_FOUT + k
                    ve.wait_ge(a_hi, i * 4 + k + 1)
                    ve.tensor_tensor(asl[:, k % 2, :], act[:, bass.ds(i * 4 + k, 1), :].rearrange("p o n -> p (o n)"),
                                     ash[:, k % 2, :].bitcast(F32), ALU.subtract).then_inc(a_lo, 1)
                    ve.wait_ge(w_hi, i * 4 + c + 1)
                    ve.tensor_tensor(wl[:, c % 2, :], raw[:, c % RAW_SLOTS, :], wh[:, c % 2, :].bitcast(F32),
                                     ALU.subtract).then_inc(w_lo_dve, 1)
            for k in range(20, NF):
                act_lo(k)
                lo(C_FOUT + k)

            def z_mean(t):
                ve.wait_ge(z_sq, 2 * t + 2)
                link(ve.tensor_tensor(stat[:, t:t + 1], stat[:, 56 + 2 * t:57 + 2 * t],
                                      stat[:, 57 + 2 * t:58 + 2 * t], ALU.add))
                ve.tensor_scalar(stat[:, 36 + t:37 + t], stat[:, t:t + 1], 1.0 / D, EPS, ALU.mult,
                                 ALU.add).then_inc(z_ms, 1)

            ve.wait_ge(wfpost_in, 16)
            z_mean(0)
            for t in range(NT):
                ve.wait_ge(z_rstd, t + 1)
                for half in range(2):
                    link(ve.scalar_tensor_tensor(out=xn[:, t % 2, 512 * half:512 * half + 512],
                                                 in0=bank[4 * half + t][:, :], scalar=stat[:, 40 + t:41 + t],
                                                 in1=wfpost[:, 512 * half:512 * half + 512], op0=ALU.mult,
                                                 op1=ALU.mult))
                if t + 1 < NT:
                    z_mean(t + 1)
                ve.tensor_tensor(x1[:, t, :], x1[:, t, :], xn[:, t % 2, :], ALU.add).then_inc(out_ready, 1)

        @block.tensor
        def _(te):
            mm = nc.tensor.matmul

            rows_done = [0]

            def other_rows(ins):
                rows_done[0] += 1
                ins.then_inc(pe_rows, 1)
                te.wait_ge(pe_rows, rows_done[0])

            def three(out, lh, ll, rh, rl, start, stop):
                mm(out, ll, rh, start=start, stop=False, skip_group_check=True)
                mm(out, lh, rl, start=False, stop=False, skip_group_check=True)
                return mm(out, lh, rh, start=False, stop=stop, skip_group_check=True)

            def feature_major(out, b, k0=0, nk=KD, xh=hh, xl=hl):
                for k in range(nk):
                    last = three(out, wh[:, b, k * P:k * P + P], wl[:, b, k * P:k * P + P], xh[:, k, :], xl[:, k, :],
                                 k == 0, k == nk - 1)
                return last

            te.wait_ge(small_in, 16)
            te.wait_ge(onehot_in, 16)
            te.wait_ge(rel_ready, 4)
            for i in range(10):
                if i >= 8:
                    te.wait_ge(table_out, i - 7)
                if i < 2:
                    for k in range(64):
                        t, n = 2 * i + k // 32, k % 32
                        d = P * t - 16 * n - 31 + D0
                        last = mm(bank[i][:, 8 * k:8 * k + 8], onehot[:, d:d + P], rel3[:, 0:8], start=True, stop=True)
                else:
                    for k in range(32):
                        d = P - (32 * (i - 2) + k) + D0
                        last = mm(bank[i % 8][:, 16 * k:16 * k + 16], onehot[:, d:d + P], rel3[:, :],
                                  start=True, stop=True)
                last.then_inc(table_full, 1)
            te.wait_ge(const_ready, 1)
            te.wait_ge(xn_ready, 4)
            te.wait_ge(table_out, 10)
            for k in range(KD):
                for t in range(NT):
                    last = te.transpose(bank[k][:, t * P:t * P + P], xs[:, t, k * P:k * P + P], ident[:, :])
                last.then_inc(xT_full, 1)

            def aux_free_for(name):
                n = AUX_AT[name]
                if n >= 2:
                    te.wait_ge(aux_free[n % 2], n // 2)
                else:
                    te.wait_ge(h_lo, 8)

            def level(l):
                for t in range(NT):
                    name = f"lv{l}_{t}"
                    aux_free_for(name)
                    if l < 7:
                        te.wait_ge(z_ready, 2 * l + 2)
                    for h in (0, 2, 1, 3):
                        b, p = 64 * (h % 2), h // 2
                        if h == 1:
                            other_rows(last)
                        cols = slice(512 * p + P * t, 512 * p + P * t + P)
                        kk = zz[b:b + 64, l % 2, cols] if l < 7 else gk[b:b + 64, cols]
                        qq = zz[b:b + 64, l % 2, cols] if l < 7 else gq[b:b + 64, cols]
                        last = mm(aux_bank(name)[:, P * h:P * h + P], kk, qq, start=True, stop=True)
                    last.then_inc(aux_done, 1)

            def token_major(c):
                kind, j = STRAIGHT[c]
                b = c % 2
                nk, width, n_j = (4, 256, 2) if kind == "nv" else (2, 512, 4)
                for t in range(NT):
                    if j == 0:
                        if TM_USE[kind]:
                            te.wait_ge(tm_free[t], TM_USE[kind])
                    for k in range(nk):
                        cols = slice(k * width, k * width + width)
                        last = three(bank[t][:, 0:width], hh[:, nk * j + k, t * P:t * P + P],
                                     hl[:, nk * j + k, t * P:t * P + P], wh[:, b, cols], wl[:, b, cols],
                                     j == 0 and k == 0, j == n_j - 1 and k == nk - 1)
                    if j == n_j - 1 and t < NT - 1:
                        last.then_inc(tm_done, 1)
                return last

            def chunk(c):
                kind, j = STRAIGHT[c]
                b = c % 2
                te.wait_ge(w_hi, c + 1)
                lo_split(te, c)
                if c == 0:
                    te.wait_ge(h_lo, KD)
                if c in SINGLE and not (kind in ("w1k", "w1v") and j == 1):
                    n = SINGLE[c]
                    if n >= 2:
                        te.wait_ge(s_free[n % 2], n // 2)
                if kind in ("ag", "blr"):
                    ps, w = single_bank(c), 24 if kind == "ag" else 16
                    for t in range(NT):
                        for k in range(KD):
                            last = three(ps[:, w * t:w * t + w], hh[:, k, t * P:t * P + P], hl[:, k, t * P:t * P + P],
                                         wh[:, b, w * k:w * k + w], wl[:, b, w * k:w * k + w], k == 0, k == KD - 1)
                elif kind in ("bv", "br", "nv", "cv"):
                    last = token_major(c)
                elif kind in ("w1k", "w1v"):
                    kv = 0 if kind == "w1k" else 1
                    ps = single_bank(c)
                    if j == 0:
                        single_out(te, slot_of("kc" if kv == 0 else "vc"))
                    for g in (j, 1 - j):
                        r = slice(64 * g, 64 * g + 64)
                        if g != j:
                            other_rows(last)
                        for k in range(16):
                            l = 16 * j + k
                            first = j == 0 and k == 0 and g == 0
                            last = three(ps[0:64, 32 * g:32 * g + 32], wh[r, b, 64 * k:64 * k + 64],
                                         wl[r, b, 64 * k:64 * k + 64], kxh[r, kv, l, :], kxl[r, kv, l, :],
                                         first, l == 31)
                else:
                    last = feature_major(single_bank(c)[:, :], b)
                last.then_inc(w_used, 1)

            for c in range(C_MERGE):
                chunk(c)
                if c == 2:
                    te.wait_ge(const_ready, 2)
                    single_out(te, 1)
                    aux_free_for("lrT")
                    for t in range(NT):
                        last = te.transpose(aux_bank("lrT")[0:16, t * P:t * P + P], lr[:, t, :], ident[:, :])
                    last.then_inc(aux_done, 1)
                if c == 3:
                    aux_out(te, "lrT")
                    for t in range(NT):
                        name = f"z{t // 2}"
                        if t % 2 == 0:
                            aux_free_for(name)
                        last = mm(aux_bank(name)[:, 256 * (t % 2):256 * (t % 2) + 256], gsq[0:16, t * P:t * P + P],
                                  small[0:16, S_W2:S_W2 + 256], start=True, stop=True)
                        if t % 2 == 1:
                            last.then_inc(aux_done, 1)
                if c == 5:
                    te.wait_ge(ls_ready, 1)
                    for p in range(2):
                        aux_free_for(f"bT{p}")
                        for t in range(NT):
                            last = mm(aux_bank(f"bT{p}")[:, t * P:t * P + P], gz[:, 256 * t + P * p:256 * t + P * p + P],
                                      tri[:, :], start=True, stop=True)
                        last.then_inc(aux_done, 1)
                if 7 <= c < 15:
                    level(c - 7)
                if c == 15:
                    te.wait_ge(kd_ready, 1)
                    for k in range(2):
                        aux_free_for(f"kd{k}")
                        for t in range(2 * k, 2 * k + 2):
                            for p in range(2):
                                last = te.transpose(aux_bank(f"kd{k}")[:, 256 * (t % 2) + P * p:256 * (t % 2) + P * p + P],
                                                    zz[:, 0, 512 * p + P * t:512 * p + P * t + P], ident[:, :])
                        last.then_inc(aux_done, 1)
                if 16 <= c < 20:
                    t = c - 16
                    aux_free_for(f"o{t}")
                    aux_out(te, f"lv7_{t}")
                    te.wait_ge(kd_ready, 2)
                    te.wait_ge(tm_free[t], 1)
                    if t == 0:
                        aux_out(te, "kd0")
                        aux_out(te, "kd1")
                    else:
                        aux_out(te, f"s{t - 1}")
                    for h in range(4):
                        last = mm(aux_bank(f"o{t}")[:, P * h:P * h + P], attnT[:, t, h, :], gv[:, t, P * h:P * h + P],
                                  start=h == 0, stop=t == 0, skip_group_check=True)
                    for h in (0, 2, 1, 3) if t > 0 else ():
                        b, p = 64 * (h % 2), h // 2
                        if h == 1:
                            other_rows(last)
                        last = mm(aux_bank(f"o{t}")[:, P * h:P * h + P],
                                  zz[b:b + 64, 1, 512 * p + P * t:512 * p + P * t + P],
                                  state[b:b + 64, p, P * (h % 2):P * (h % 2) + P], start=False, stop=True,
                                  skip_group_check=True)
                    last.then_inc(aux_done, 1)
                    if t < 3:
                        aux_free_for(f"s{t}")
                        for p in range(2):
                            last = mm(aux_bank(f"s{t}")[:, 256 * p:256 * p + 256],
                                      gz[:, 256 * t + P * p:256 * t + P * p + P], gv[:, t, 256 * p:256 * p + 256],
                                      start=True, stop=True)
                        last.then_inc(aux_done, 1)
                if c == 20:
                    for t in range(NT):
                        te.wait_ge(tm_free[t], TM_USE["ot"])
                        aux_out(te, f"o{t}")
                        for h in range(4):
                            last = te.transpose(bank[t][:, P * h:P * h + P], gr[:, t, P * h:P * h + P], ident[:, :])
                        last.then_inc(ot_full, 1)
                if c == 21:
                    te.wait_ge(hid_ready, 1)
                    aux_free_for("cmp")
                    ps = aux_bank("cmp")
                    mm(ps[0:64, 0:64], small[0:64, S_CK2:S_CK2 + 64], ghid[:, 5, 0:64], start=True, stop=True)
                    mm(ps[0:64, 64:128], ghid[:, 5, 64:128], small[0:64, S_CV2:S_CV2 + 64], start=True,
                       stop=True).then_inc(aux_done, 1)
                if c == FIRST_MOBA - 1:
                    compressed_scores_pe(te, three, other_rows)
                if c == CMP_BACK:
                    compressed_transposes(te)

            attention_pe(te, mm, three)

            branch = [(oah, oal), (obh, obl), (och, ocl)]
            with te.Fori(0, 4) as i:
                for s in range(6):
                    c = C_MERGE + 2 * s
                    te.wait_ge(d_free, i * 6 + s + 1)
                    te.wait_ge(w_hi, i * 12 + c + 1)
                    te.wait_ge(w_lo_dve, i * 12 + c + 1 - C_MERGE)
                    feature_major(bank[s % 2][:, :], 0).then_inc(w_used, 1)
                    te.wait_ge(w_hi, i * 12 + c + 2)
                    te.wait_ge(w_lo_dve, i * 12 + c + 2 - C_MERGE)
                    xh, xl = branch[s % 3]
                    if s % 3 == 0:
                        te.wait_ge(head_lo, 8)
                    if s % 3 == 2:
                        te.wait_ge(head_lo, 16)
                    feature_major(bank[2 + s % 2][:, :], 1, nk=4, xh=xh, xl=xl).then_inc(w_used, 1)
            te.wait_ge(d_ml, 8)
            for m in range(8):
                c = C_OUT + m
                half, q = m // 4, m % 4
                te.wait_ge(w_hi, c + 1)
                lo_split(te, c)
                if m == 4:
                    te.wait_ge(d_free, 26)
                for t in range(NT):
                    for k in range(2):
                        kk = 2 * q + k
                        cols = slice(512 * k, 512 * k + 512)
                        last = three(bank[4 * (1 - half) + t][:, :], meh[:, kk, t * P:t * P + P],
                                     mel[:, kk, t * P:t * P + P], wh[:, c % 2, cols], wl[:, c % 2, cols],
                                     q == 0 and k == 0, q == 3 and k == 1)
                    if m == 7 and t < NT - 1:
                        last.then_inc(y_full, 1)
                last.then_inc(w_used, 1)
            for t in range(NT):
                te.wait_ge(n_ready, t + 1)
                for half in range(2):
                    for k in range(4):
                        last = te.transpose(bank[4 * half + t][:, k * P:k * P + P],
                                            xn[:, t % 2, (4 * half + k) * P:(4 * half + k) * P + P], ident[:, :])
                    last.then_inc(n_T, 1)
            te.wait_ge(n_lo, 8)
            with te.Fori(0, NF // 2) as i:
                for f in range(2):
                    te.wait_ge(f_free, i * 2 + f + 1)
                    for part in range(2):
                        c = C_FIN + 2 * f + part
                        te.wait_ge(w_hi, i * 4 + c + 1)
                        te.wait_ge(w_lo_dve, i * 4 + c + 1 - C_MERGE)
                        feature_major(bank[2 * f + part][:, :], c % 2).then_inc(w_used, 1)

            def down(k, t, start, stop):
                b = k % 2
                for half in range(2):
                    cols = slice(512 * half, 512 * half + 512)
                    last = three(bank[4 * half + t][:, :], ash[:, b, t * P:t * P + P], asl[:, b, t * P:t * P + P],
                                 wh[:, b, cols], wl[:, b, cols], start, stop)
                return last

            for k in range(2):
                te.wait_ge(w_hi, C_FOUT + k + 1)
                lo_split(te, C_FOUT + k)
                te.wait_ge(a_hi, k + 1)
                te.wait_ge(a_lo, k + 1)
                if k == 0:
                    te.wait_ge(f_free, NF + 2)
                for t in range(NT):
                    last = down(k, t, k == 0, False)
                last.then_inc(w_used, 1)
            with te.Fori(0, 4) as i:
                for k in range(2, 6):
                    te.wait_ge(w_hi, i * 4 + C_FOUT + k + 1)
                    te.wait_ge(w_lo_dve, i * 4 + C_FOUT + k + 1 - C_MERGE)
                    te.wait_ge(a_hi, i * 4 + k + 1)
                    te.wait_ge(a_lo, i * 4 + k + 1)
                    for t in range(NT):
                        last = down(k, t, False, False)
                    last.then_inc(w_used, 1)
            for k in range(18, 20):
                te.wait_ge(w_hi, C_FOUT + k + 1)
                lo_split(te, C_FOUT + k)
                te.wait_ge(a_hi, k + 1)
                te.wait_ge(a_lo, k + 1)
                for t in range(NT):
                    last = down(k, t, False, False)
                last.then_inc(w_used, 1)
            te.wait_ge(w_hi, N_CHUNKS)
            lo_split(te, N_CHUNKS - 1)
            te.wait_ge(a_hi, NF)
            te.wait_ge(a_lo, NF)
            for t in range(NT):
                down(NF - 2, t, False, False)
                down(NF - 1, t, False, True).then_inc(z_full, 1)



def bucket_of(distance):
    n = np.maximum(distance, 1).astype(np.float32)
    large = 16 + (np.log(n / np.float32(16)) / np.float32(np.log(8.0)) * 16).astype(np.int32)
    return np.where(distance < 16, distance, np.minimum(large, 31))


def distance_onehot():
    d = np.arange(D_TABLE) - D0
    table = np.zeros((97, D_TABLE), np.uint16)
    for k in range(3):
        cols = np.nonzero(d >= 0)[0]
        table[32 * k + bucket_of(d[cols]), cols] = 0x3F80
    table[96, d < 0] = 0x3F80
    return table


def level_masks():
    j, i = np.arange(P)[:, None], np.arange(P)[None, :]
    masks = [(i // (2 * s) == j // (2 * s)) & (j // s % 2 == 0) & (i // s % 2 == 1) for s in LEVELS] + [i == j]
    return np.ascontiguousarray(np.stack(masks, 1).astype(np.uint16))


def pack_weights(a):
    w, out = a["w_in"][0], []
    packed = np.zeros((N_CHUNKS, P, CHUNK), np.float32)

    def tiles(m):
        k, n = m.shape
        return m.reshape(k // P, P, n).transpose(1, 0, 2).reshape(P, k // P * n)

    cols = {"bq": (B_Q, P), "bk": (B_K, P), "kc": (A_KC, P), "vc": (A_VC, P), "ks": (A_KS, P), "kw": (A_KW, P),
            "cq": (C_Q, P), "ck": (C_K, P), "ag": (A_G, 24), "blr": (B_LR, 16)}
    for kind, j in STRAIGHT:
        if kind in cols:
            at, n = cols[kind]
            out.append(tiles(w[:, at + n * j:at + n * j + n]))
        elif kind == "aq":
            out.append(tiles(np.concatenate([w[:, 64 * j:64 * j + 64], w[:, 64 * (j + 4):64 * (j + 4) + 64]], 1)))
        elif kind in ("bv", "br", "cv"):
            at = {"bv": B_V, "br": B_R, "cv": C_V}[kind]
            out.append(tiles(w[256 * j:256 * j + 256, at:at + 512]))
        elif kind == "nv":
            rows = w[512 * j:512 * j + 512]
            out.append(tiles(np.concatenate([rows[:, A_VS:A_VS + P], rows[:, A_VW:A_VW + P]], 1)))
        else:
            m = a["nsa_cmp_k_w1" if kind == "w1k" else "nsa_cmp_v_w1"][0]
            m = m.reshape(32, 64, 64)[16 * j:16 * j + 16].transpose(1, 0, 2).reshape(64, CHUNK)
            out.append(np.concatenate([m, m], 0))
    for n in range(KD):
        for b, name in enumerate(("w_branch_a", "w_branch_b", "w_branch_c")):
            out.append(tiles(w[:, M_G + D * b + P * n:M_G + D * b + P * n + P]))
            rows = a[name][0][:, P * n:P * n + P]
            if b == 0:
                rows = rows.reshape(2, 4, 64, P).transpose(1, 0, 2, 3).reshape(512, P)
            out.append(tiles(rows))
    for half in range(2):
        for q in range(4):
            out.append(tiles(a["w_out"][0][256 * q:256 * q + 256, 512 * half:512 * half + 512]))
    for f in range(NF):
        for side in range(2):
            out.append(tiles(a["w_ffn_in"][0][:, HID * side + P * f:HID * side + P * f + P]))
    for k in range(NF):
        out.append(a["w_ffn_out"][0][P * k:P * k + P])
    for c, m in enumerate(out):
        packed[c, :, :m.shape[1]] = m
    return packed


def pack_small(a):
    s = np.zeros((P, S_END), np.float32)
    s[:, S_GNORM] = a["gla_norm"][0]
    s[:, S_GB:S_GB + 256] = a["gla_gate_b"][0][None, :]
    s[0:16, S_W2:S_W2 + 256] = a["gla_gate_w2"][0]
    for k in range(3):
        s[32 * k:32 * k + 32, S_REL:S_REL + 16] = a["rel_bias"]
    for g in range(2):
        s[64 * g:64 * g + 64, S_PEK:S_PEK + 32] = a["nsa_pe_k"][0].T
        s[64 * g:64 * g + 64, S_PEV:S_PEV + 32] = a["nsa_pe_v"][0].T
    s[0:64, S_CK2:S_CK2 + 64] = a["nsa_cmp_k_w2"][0]
    s[0:64, S_CV2:S_CV2 + 64] = a["nsa_cmp_v_w2"][0]
    return s


def kernel(**inputs):
    import concourse.bacc as bacc
    from concourse.bass_utils import run_bass_kernel_spmd

    a = {k: np.asarray(v) for k, v in inputs.items()}
    rows = np.stack([np.broadcast_to(a[n][0], (P, D)) for n in
                     ("norm_mix_pre", "norm_mix_post", "norm_ffn_pre", "norm_ffn_post")])
    arrays = {"wpack": pack_weights(a), "small_params": pack_small(a), "norm_rows": np.ascontiguousarray(rows),
              "distance_onehot": distance_onehot(), "level_masks": level_masks(),
              "x_in": np.ascontiguousarray(a["x"][0])}
    nc = bacc.Bacc("TRN2", target_bir_lowering=False, num_devices=1)
    args = [nc.dram_tensor(n, v.shape, mybir.dt.from_np(v.dtype), kind="ExternalInput").ap()
            for n, v in arrays.items()]
    args.append(nc.dram_tensor("x_out", (1, SEQ, D), F32, kind="ExternalOutput").ap())
    program(nc, *args)
    return run_bass_kernel_spmd(nc, [arrays], core_ids=[0]).results[0]["x_out"]
```

```python
from contextlib import ExitStack

import numpy as np

import concourse.bass as bass
from concourse import mybir

F32 = mybir.dt.float32
F32R = mybir.dt.float32r
BF16 = mybir.dt.bfloat16
U16 = mybir.dt.uint16
U8 = mybir.dt.uint8
ALU = mybir.AluOpType
ACT = mybir.ActivationFunctionType
AX = mybir.AxisListType

P = 128
SEQ, D = 512, 1024
NT = SEQ // P
KD = D // P
HID = 2816
NF = HID // P
EPS = 1e-6
MASKED = -1e30
CHUNK = 1024
RAW_SLOTS, SPLIT_SLOTS = 4, 2

A_Q, A_KC, A_VC, A_KS, A_VS, A_KW, A_VW, A_G = 0, 512, 640, 768, 896, 1024, 1152, 1280
B_Q, B_K, B_V, B_R, B_LR = 1304, 1560, 1816, 2328, 2840
C_Q, C_K, C_V, M_G = 2856, 3368, 3880, 4392

STRAIGHT = ([("agl", 0), ("bq", 0), ("bq", 1), ("bk", 0), ("bk", 1)]
            + [("bv", j) for j in range(4)] + [("br", j) for j in range(4)]
            + [("kc", 0), ("vc", 0), ("w1k", 0), ("w1v", 0), ("ks", 0), ("kw", 0), ("aq", 0), ("aq", 1)]
            + [("nv", 0), ("nv", 1), ("aq", 2), ("aq", 3)]
            + [("cq", j) for j in range(4)] + [("ck", j) for j in range(4)] + [("cv", j) for j in range(4)])
C_MERGE = len(STRAIGHT)
C_OUT = C_MERGE + 8 * 6
C_FIN = C_OUT + 8
C_FOUT = C_FIN + 2 * NF
N_CHUNKS = C_FOUT + NF
WIDTH = {"agl": KD * 64}
FIRST_MOBA = STRAIGHT.index(("cq", 0))
CMP_BACK = FIRST_MOBA + 4

S_GNORM, S_GB, S_W2, S_REL, S_PEK, S_PEV, S_CK2, S_CV2, S_PRE, S_END = 0, 1, 257, 513, 529, 561, 593, 657, 721, 729
D0, D_TABLE = 544, 1056
GELU_1 = 2 * (2 / np.pi) ** 0.5
GELU_3 = GELU_1 * 0.044715
SBUF_BASE = 16512
KX_PARTS = [(odd, g) for odd in range(2) for g in range(2)]
LEVELS = [64, 32, 16, 8, 4, 2, 1]


def single_bank_chunks():
    index = {}
    for c, (kind, j) in enumerate(STRAIGHT):
        if kind not in ("bv", "br", "nv", "cv"):
            index[c] = len(index)
    return index


SINGLE = single_bank_chunks()
TM_USE = {"bv": 0, "br": 1, "ot": 2, "nv": 3, "cv": 4}
AUX = (["gates", "z0", "z1", "bT0", "bT1"] + [f"lv{l}_{t}" for l in range(8) for t in range(NT)]
       + ["kd0", "kd1", "o0", "s0", "o1", "s1", "o2", "s2", "o3", "cmp"])
AUX_AT = {name: i for i, name in enumerate(AUX)}
TILE_ORDER = (3, 0, 2, 1)
NSA_UNITS = [(br, 4 * g + p, i) for p in range(4) for g in range(2) for i in TILE_ORDER for br in ("s", "w")]
MOBA_UNITS = [("m", h, i) for h in range(8) for i in TILE_ORDER]
UNITS = NSA_UNITS + MOBA_UNITS
N_NSA = len(NSA_UNITS)
T_LAG, PV_LAG = 6, 8
STEPS = len(UNITS) + PV_LAG + 2


def program(nc, wpack, small_d, rows_d, onehot_d, mask_d, x_d, out_d):
    ctx = ExitStack()
    with ctx:
        def sem(name):
            return ctx.enter_context(nc.semaphore(name))

        bank = [ctx.enter_context(nc.psum_tensor(f"bank{i}", [P, 512], F32)) for i in range(8)]

        def at(kib, name, shape, dt=F32):
            return nc.alloc_sbuf_tensor_at(name, shape, dt, offset=int(SBUF_BASE + kib * 1024))

        hh = at(0, "h_hi", [P, KD, SEQ], F32R)
        hl = at(16, "h_lo", [P, KD, SEQ], F32R)
        raw = at(32, "w_raw", [P, RAW_SLOTS, CHUNK])
        wh = at(48, "w_hi", [P, SPLIT_SLOTS, CHUNK], F32R)
        wl = at(56, "w_lo", [P, SPLIT_SLOTS, CHUNK], F32R)
        small = at(64, "small", [P, S_END])
        ident = at(67, "ident", [P, P])
        tri = at(67.5, "tri", [P, P])
        lmask = at(106, "lmask", [P, 8, P], U16)
        gate = at(69, "gate", [P, NT, 24])
        stat = at(69.5, "stat", [P, 96])
        minus_half = at(69.875, "minus_half", [P, 4])
        gsq = at(70, "gsq", [P, 512])
        obh = at(72, "ob_hi", [P, 4, SEQ], F32R)
        obl = at(80, "ob_lo", [P, 4, SEQ], F32R)
        band = at(88, "band", [P, 16, 256])
        fullb = at(104, "fullb", [P, 2, 512])
        ghid = at(104, "ghid", [64, 6, P])
        cmpb = at(108, "cmpb", [P, NT, 8, 32])
        xs = at(112, "xs", [P, NT, D])
        onehot = at(128, "onehot", [97, D_TABLE], BF16)
        rel3 = at(136, "rel3", [97, 16], BF16)
        relb = at(136.25, "relb", [96, 3, 16], BF16)
        relr = at(136.5, "relr", [96, 2, 16])
        aqh = at(112, "aq_hi", [P, 4, SEQ], F32R)
        aql = at(120, "aq_lo", [P, 4, SEQ], F32R)
        akh = at(128, "ak_hi", [P, 2, SEQ], F32R)
        akl = at(132, "ak_lo", [P, 2, SEQ], F32R)
        av = at(136, "av", [P, NT, 256])
        kxh = at(140, "kx_hi", [P, 2, 8, 68], F32R)
        kxl = at(146, "kx_lo", [P, 2, 8, 68], F32R)
        gq = at(156, "gq", [P, 1024])
        gk = at(160, "gk", [P, 1024])
        gv = at(164, "gv", [P, NT, 512])
        gr = at(172, "gr", [P, NT, 512])
        gz = at(180, "gz", [P, 1024])
        zz = at(184, "zz", [P, 2, 1024])
        bT = at(192, "bT", [P, 1024])
        attnT = at(196, "attnT", [P, NT, 4, P])
        state = at(204, "state", [P, 2, 256])
        ebl = at(206.5, "ebl", [P, 8])
        pcs = at(188, "pcs", [P, NT * 8, 32])
        pcT = at(192, "pcT", [P, NT, 256])
        csT = at(164, "csT", [P, 2, 512])
        sc = at(164, "sc", [P, 8, 512])
        pT = [at(188, "pT0", [P, 512]), at(190, "pT1", [P, 512]), at(70, "pT2", [P, 512])]
        oah = at(112, "oa_hi", [P, 4, SEQ], F32R)
        oal = at(120, "oa_lo", [P, 4, SEQ], F32R)
        ckh = at(151, "ck_hi", [P, 640], F32R)
        ckl = at(153.5, "ck_lo", [P, 640], F32R)
        cvv = at(204.25, "cvv", [P, 2, 64])
        ast = at(204.75, "ast", [P, 8, 4])
        cst = at(205, "cst", [P, 4, 32])
        cqh = at(140, "cq_hi", [P, 4, SEQ], F32R)
        cql = at(148, "cq_lo", [P, 4, SEQ], F32R)
        kmh = at(180, "ckey_hi", [P, 4, SEQ], F32R)
        kml = at(196, "ckey_lo", [P, 4, SEQ], F32R)
        cv = at(156, "cv", [P, NT, 512])
        och = at(140, "oc_hi", [P, 4, SEQ], F32R)
        ocl = at(148, "oc_lo", [P, 4, SEQ], F32R)
        meh = at(156, "me_hi", [P, KD, SEQ], F32R)
        mel = at(172, "me_lo", [P, KD, SEQ], F32R)
        sig = at(188, "sig", [P, 2, SEQ])
        mrg = at(192, "mrg", [P, 2, SEQ])
        prod = at(196, "prod", [P, SEQ])
        xr = at(88, "xr", [P, NT, D])
        wpost = at(104, "wpost", [P, D])
        wfpre = at(108, "wfpre", [P, D])
        x1 = at(128, "x1", [P, NT, D])
        xn = at(144, "xn", [P, 2, D])
        junk = at(152, "junk", [P, 512])
        wfpost = at(160, "wfpost", [P, D])
        act = at(72, "act", [P, NF, SEQ])
        ash = at(116, "as_hi", [P, 2, SEQ], F32R)
        asl = at(120, "as_lo", [P, 2, SEQ], F32R)
        silu = at(124, "silu", [P, 2, SEQ])

        small_in, onehot_in, mask_in = sem("small_in"), sem("onehot_in"), sem("mask_in")
        x_in = [sem(f"x_in{t}") for t in range(NT)]
        xr_in, posts_in, wfpost_in, stored = sem("xr_in"), sem("posts_in"), sem("wfpost_in"), sem("stored")
        w_in = [sem(f"w_in{s}") for s in range(RAW_SLOTS)]
        w_hi = sem("w_hi")
        w_lo_pool, w_lo_dve = sem("w_lo_pool"), sem("w_lo_dve")
        w_used = sem("w_used")
        const_ready, zeros_ready = sem("const_ready"), sem("zeros_ready")
        dchain = sem("dchain")
        rel_ready, table_full, table_out = sem("rel_ready"), sem("table_full"), sem("table_out")
        sq_act, ms_ready, rstd_ready, xn_ready = sem("sq_act"), sem("ms_ready"), sem("rstd_ready"), sem("xn_ready")
        xn_act = sem("xn_act")
        xT_full, h_hi, h_lo = sem("xT_full"), sem("h_hi"), sem("h_lo")
        s_free = [sem("s_free4"), sem("s_free5")]
        s_hi = sem("s_hi")
        tm_done, tm_exp = sem("tm_done"), sem("tm_exp")
        tm_free = [sem(f"tm_free{t}") for t in range(NT)]
        aux_done = sem("aux_done")
        aux_free = [sem("aux_free6"), sem("aux_free7")]
        gate_ready, pe_col = sem("gate_ready"), sem("pe_col")
        softplus, ls_ready = sem("softplus"), sem("ls_ready")
        e_ready, ex_ready, z_ready = sem("e_ready"), sem("ex_ready"), sem("z_ready")
        kd_ready, o_sq, o_ms, o_rstd = sem("kd_ready"), sem("o_sq"), sem("o_ms"), sem("o_rstd")
        state_ready, o_ready, ot_hi = sem("state_ready"), sem("o_ready"), sem("ot_hi")
        ot_full = sem("ot_full")
        hid_u, hid_e, hid_ready, cmp_ready = sem("hid_u"), sem("hid_e"), sem("hid_ready"), sem("cmp_ready")
        cs_raw, cs_copied = sem("cs_raw"), sem("cs_copied")
        cs_full, cs_sub, cs_exp, cs_prob, cs_tr, cs_T = (sem("cs_full"), sem("cs_sub"), sem("cs_exp"),
                                                         sem("cs_prob"), sem("cs_tr"), sem("cs_T"))
        bias_ready, s_full, s_max, s_exp = sem("bias_ready"), sem("s_full"), sem("s_max"), sem("s_exp")
        s_rcp, s_prob, t_full, pv_done = sem("s_rcp"), sem("s_prob"), sem("t_full"), sem("pv_done")
        t_out = [sem("t_out_act"), sem("t_out_dve")]
        head_hi, head_lo = sem("head_hi"), sem("head_lo")
        d_sig, d_free, d_acc, d_mh, d_ml = sem("d_sig"), sem("d_free"), sem("d_acc"), sem("d_mh"), sem("d_ml")
        y_full, y_sq, y_ms, y_rstd, x1_ready = sem("y_full"), sem("y_sq"), sem("y_ms"), sem("y_rstd"), sem("x1_ready")
        x_sq, x_ms, x_rstd, n_ready, n_T = sem("x_sq"), sem("x_ms"), sem("x_rstd"), sem("n_ready"), sem("n_T")
        n_hi, n_lo = sem("n_hi"), sem("n_lo")
        f_sig, f_free, a_hi, a_lo = sem("f_sig"), sem("f_free"), sem("a_hi"), sem("a_lo")
        z_full, z_sq, z_ms, z_rstd, out_ready = (sem("z_full"), sem("z_sq"), sem("z_ms"), sem("z_rstd"),
                                                 sem("out_ready"))
        pe_rows = sem("pe_rows")
        block = ctx.enter_context(nc.Block())

        def landed(eng, slot, turn):
            eng.wait_ge(w_in[slot], 16 * (turn + 1))

        def lo_split(eng, c):
            if c < C_MERGE:
                eng.wait_ge(w_lo_pool, c + 1)
            else:
                eng.wait_ge(w_lo_dve, c + 1 - C_MERGE)

        def single_out(eng, c):
            eng.wait_ge(s_free[SINGLE[c] % 2], SINGLE[c] // 2 + 1)

        def tile_done(eng, c, group, t):
            if t < NT - 1:
                eng.wait_ge(tm_done, 3 * group + t + 1)
            else:
                eng.wait_ge(w_used, c + 1)

        def y_tile_done(eng, t):
            if t < NT - 1:
                eng.wait_ge(y_full, t + 1)
            else:
                eng.wait_ge(w_used, C_OUT + 8)

        def aux_full(eng, name):
            eng.wait_ge(aux_done, AUX_AT[name] + 1)

        def aux_out(eng, name):
            eng.wait_ge(aux_free[AUX_AT[name] % 2], AUX_AT[name] // 2 + 1)

        def aux_bank(name):
            return bank[6 + AUX_AT[name] % 2]

        def kx_part(kx, ps, kv, odd, g):
            return (kx[64 * odd:64 * odd + 64, kv, :, 32 * g:32 * g + 32],
                    ps[64 * g:64 * g + 64, :].rearrange("p (n l o) -> p l n o", l=8, o=2)[:, :, :, odd])

        def pe_cols(kv):
            at_ = (S_PEK, S_PEV)[kv]
            return small[:, at_:at_ + 32].rearrange("p (l c) -> p l c", c=4)

        def input_bank(k):
            return bank[(k + 4) % 8]

        def single_bank(c):
            return bank[4 + SINGLE[c] % 2]

        def slot_of(kind, j=0):
            return STRAIGHT.index((kind, j))

        def qkv(u):
            br, h, i = UNITS[u]
            if br == "m":
                b, p = 64 * (h % 2), h // 2
                return (cqh[b:b + 64, p], cql[b:b + 64, p], kmh[b:b + 64, p], kml[b:b + 64, p],
                        cv[:, :, 64 * h:64 * h + 64])
            g, p, s = h // 4, h % 4, 0 if br == "s" else 1
            b = 64 * g
            return (aqh[b:b + 64, p], aql[b:b + 64, p], akh[b:b + 64, s], akl[b:b + 64, s],
                    av[:, :, 128 * s + 64 * g:128 * s + 64 * g + 64])

        def head_of(u):
            if u < N_NSA:
                return u // 8, u % 8 == 0, u % 8 == 7
            return 8 + (u - N_NSA) // 4, u % 4 == 0, u % 4 == 3

        def score_bank(u):
            return bank[(0, 1, 6, 7)[u % 4]]

        def bias_head(n):
            return UNITS[8 * n][1] if n < 8 else n

        def output_bank(n):
            b = 64 * (n % 2)
            return bank[4 + n % 2][b:b + 64, :]

        def head_rows(n):
            hi_, lo_ = (oah, oal) if n < 8 else (och, ocl)
            b, p = 64 * (n % 2), n % 8 // 2
            return hi_[b:b + 64, p, :], lo_[b:b + 64, p, :]

        def level_view(ap, s):
            return ap.rearrange("p (n u s) -> p n u s", u=2, s=s)

        def transposed_hi(sa, t):
            for half in range(2):
                sa.wait_ge(n_T, 2 * t + half + 1)
                sa.activation(hh[:, 4 * half:4 * half + 4, P * t:P * t + P],
                              bank[4 * half + t][:, :].rearrange("p (k c) -> p k c", k=4),
                              ACT.Copy).then_inc(n_hi, 1)

        def attention_act(sa):
            for u in range(STEPS):
                if u < len(UNITS):
                    n = P * (UNITS[u][2] + 1)
                    sa.wait_ge(s_max, u + 1)
                    sa.activation(sc[:, u % 8, 0:n], sc[:, u % 8, 0:n], ACT.Exp, bias=ast[:, u % 8, 0:1],
                                  scale=-1.0, accum_out=ast[:, u % 8, 1:2]).then_inc(s_exp, 1)
                v = u - T_LAG
                if 0 <= v < len(UNITS) and v % 2 == 0:
                    n = P * (UNITS[v][2] + 1)
                    sa.wait_ge(t_full, v + 1)
                    if v >= 3:
                        sa.wait_ge(pv_done, v - 2)
                    sa.activation(pT[v % 3][:, 0:n], bank[2][:, 0:n], ACT.Copy).then_inc(t_out[0], 1)
                v = u - PV_LAG - 1
                if 0 <= v < len(UNITS) and head_of(v)[2]:
                    n = head_of(v)[0]
                    sa.wait_ge(pv_done, v + 1)
                    sa.activation(head_rows(n)[0], output_bank(n), ACT.Copy).then_inc(head_hi, 1)

        def transposed_lo(ve, t):
            for half in range(2):
                ve.wait_ge(n_hi, 2 * t + half + 1)
                ve.tensor_tensor(hl[:, 4 * half:4 * half + 4, P * t:P * t + P],
                                 bank[4 * half + t][:, :].rearrange("p (k c) -> p k c", k=4),
                                 hh[:, 4 * half:4 * half + 4, P * t:P * t + P].bitcast(F32),
                                 ALU.subtract).then_inc(n_lo, 1)

        def compressed_scores(ve, link):
            for t in range(NT):
                ve.wait_ge(cs_full, t // 2 + 1)
                ins = ve.tensor_tensor(pcs[:, 8 * t:8 * t + 8, :], bank[6 + t // 2][:, 256 * (t % 2):256 * (t % 2) + 256]
                                       .rearrange("p (h n) -> p h n", h=8), cmpb[:, t, :, :], ALU.add)
                link(ins)
            link(ve.tensor_reduce(cst[:, 0, :], pcs[:, :, :], AX.X, ALU.max))
            link(ve.tensor_scalar(cst[:, 0, :], cst[:, 0, :], -1e29, None, ALU.max))
            ve.tensor_tensor(pcs[:, :, :], pcs[:, :, :], cst[:, 0, :].unsqueeze(2).broadcast_to([P, 32, 32]),
                             ALU.subtract).then_inc(cs_sub, 1)
            ve.wait_ge(cs_exp, 1)
            link(ve.tensor_reduce(cst[:, 1, :], pcs[:, :, :], AX.X, ALU.add))
            link(ve.tensor_scalar(cst[:, 1, :], cst[:, 1, :], 1e-20, None, ALU.max))
            link(ve.reciprocal(cst[:, 2, :], cst[:, 1, :]))
            ve.wait_ge(gate_ready, 1)
            link(ve.tensor_tensor(cst[:, 3, :].rearrange("p (t h) -> p t h", t=NT),
                                  cst[:, 2, :].rearrange("p (t h) -> p t h", t=NT),
                                  gate[:, :, :].rearrange("p t (h b) -> p t h b", b=3)[:, :, :, 0], ALU.mult))
            ve.tensor_tensor(pcs[:, :, :], pcs[:, :, :], cst[:, 3, :].unsqueeze(2).broadcast_to([P, 32, 32]),
                             ALU.mult).then_inc(cs_prob, 1)

        def attention_dve(ve, link):
            def full_bias(n):
                h = bias_head(n)
                ve.tensor_copy(fullb[:, n % 2, 0:256], band[:, h, 0:1].broadcast_to([P, 256])).then_inc(bias_ready, 1)
                ve.tensor_copy(fullb[:, n % 2, 256:512], band[:, h, :]).then_inc(bias_ready, 1)

            full_bias(0)
            for u in range(STEPS):
                if u < len(UNITS):
                    n = P * (UNITS[u][2] + 1)
                    k, first, _ = head_of(u)
                    ve.wait_ge(s_full, u + 1)
                    if u >= 8:
                        ve.wait_ge(t_full, u - 7)
                    if first:
                        ve.wait_ge(bias_ready, 2 * k + 2)
                    ve.tensor_tensor_reduce(sc[:, u % 8, 0:n], score_bank(u)[:, 0:n], fullb[:, k % 2, 512 - n:512],
                                            -1.0, 3e38, ALU.add, ALU.min, ast[:, u % 8, 0:1]).then_inc(s_max, 1)
                    if first and k + 1 < 16:
                        if k > 0:
                            ve.wait_ge(s_max, u)
                        full_bias(k + 1)
                v = u - 2
                if 0 <= v < len(UNITS):
                    br, h, i = UNITS[v]
                    ve.wait_ge(s_exp, v + 1)
                    if br == "m":
                        ve.reciprocal(ast[:, v % 8, 2:3], ast[:, v % 8, 1:2]).then_inc(s_rcp, 1)
                    else:
                        g = 3 * h + (1 if br == "s" else 2)
                        link(ve.reciprocal(ast[:, v % 8, 3:4], ast[:, v % 8, 1:2]))
                        ve.tensor_tensor(ast[:, v % 8, 2:3], ast[:, v % 8, 3:4], gate[:, i, g:g + 1],
                                         ALU.mult).then_inc(s_rcp, 1)
                v = u - T_LAG
                if 0 <= v < len(UNITS) and v % 2 == 1:
                    n = P * (UNITS[v][2] + 1)
                    ve.wait_ge(t_full, v + 1)
                    if v >= 3:
                        ve.wait_ge(pv_done, v - 2)
                    ve.tensor_copy(pT[v % 3][:, 0:n], bank[3][:, 0:n]).then_inc(t_out[1], 1)
                    if v == len(UNITS) - 1:
                        ve.wait_ge(t_out[0], len(UNITS) // 2)
                        ve.engine_nop().then_inc(d_free, 2)
                v = u - PV_LAG - 2
                if 0 <= v < len(UNITS) and head_of(v)[2]:
                    n = head_of(v)[0]
                    hi_, lo_ = head_rows(n)
                    ve.wait_ge(head_hi, n + 1)
                    ve.tensor_tensor(lo_, output_bank(n), hi_.bitcast(F32), ALU.subtract).then_inc(head_lo, 1)

        def compressed_scores_pe(te, three):
            te.wait_ge(cmp_ready, 8)
            single_out(te, slot_of("aq", 3))
            single_out(te, slot_of("aq", 2))
            for g in range(2):
                r = slice(64 * g, 64 * g + 64)
                for p in range(4):
                    last = three(bank[6 + g][:, :], ckh[r, P * p:P * p + P], ckl[r, P * p:P * p + P], aqh[r, p, :],
                                 aql[r, p, :], p == 0, p == 3)
                last.then_inc(cs_raw, 1)

        def compressed_to_queries(te):
            for t in range(NT):
                te.wait_ge(cs_copied, 2)
                for g in range(2):
                    last = te.transpose(bank[6 + t // 2][:, 256 * (t % 2) + P * g:256 * (t % 2) + P * g + P],
                                        csT[:, g, P * t:P * t + P], ident[:, :])
                if t % 2 == 1:
                    last.then_inc(cs_full, 1)

        def compressed_transposes(te):
            te.wait_ge(cs_prob, 1)
            for k in range(2):
                for t in range(2 * k, 2 * k + 2):
                    for g in range(2):
                        last = te.transpose(bank[6 + k][:, (2 * (t % 2) + g) * P:(2 * (t % 2) + g) * P + P],
                                            pcs[:, 8 * t + 4 * g:8 * t + 4 * g + 4, :].rearrange("p h n -> p (h n)"),
                                            ident[:, :])
                last.then_inc(cs_tr, 1)

        def attention_pe(te, mm, three):
            for t in range(NT):
                te.wait_ge(tm_free[t], 5)
            single_out(te, slot_of("ck", 3))
            single_out(te, slot_of("ck", 2))
            for u in range(STEPS):
                if u < len(UNITS):
                    br, h, i = UNITS[u]
                    qh, ql, kh, kl, _ = qkv(u)
                    n, cols = P * (i + 1), slice(P * i, P * i + P)
                    if u == 2:
                        te.wait_ge(cs_T, 2)
                    if u >= 4:
                        te.wait_ge(s_max, u - 3)
                    three(score_bank(u)[:, 0:n], qh[:, cols], ql[:, cols], kh[:, 0:n], kl[:, 0:n], True,
                          True).then_inc(s_full, 1)
                v = u - T_LAG
                if 0 <= v < len(UNITS):
                    te.wait_ge(s_prob, v + 1)
                    if v >= 2:
                        te.wait_ge(t_out[v % 2], v // 2)
                    for j in range(UNITS[v][2] + 1):
                        last = te.transpose(bank[2 + v % 2][:, P * j:P * j + P], sc[:, v % 8, P * j:P * j + P],
                                            ident[:, :])
                    last.then_inc(t_full, 1)
                v = u - PV_LAG
                if 0 <= v < len(UNITS):
                    br, h, i = UNITS[v]
                    values = qkv(v)[4]
                    n, first, _ = head_of(v)
                    if first and n >= 2:
                        te.wait_ge(head_lo, n - 1)
                    te.wait_ge(t_out[v % 2], v // 2 + 1)
                    out = output_bank(n)[:, P * i:P * i + P]
                    for j in range(i + 1):
                        last = mm(out, values[:, j, :], pT[v % 3][:, P * j:P * j + P], start=j == 0 and br != "w",
                                  stop=j == i and br == "m", skip_group_check=True)
                    if br == "w":
                        g, r = h // 4, 32 * (h % 4)
                        last = mm(out, cvv[r:r + 32, g, :], pcT[r:r + 32, i, g * P:g * P + P], start=False, stop=True,
                                  skip_group_check=True)
                    last.then_inc(pv_done, 1)

        @block.sync
        def _(sp):
            sp.dma_start(small[:, :], small_d[:, :]).then_inc(small_in, 16)
            for t in range(NT):
                sp.dma_start(xs[:, t, :], x_d[t * P:(t + 1) * P, :]).then_inc(x_in[t], 16)

            def fetch(c):
                if c >= RAW_SLOTS:
                    sp.wait_ge(w_hi, c - RAW_SLOTS + 1)
                    lo_split(sp, c - RAW_SLOTS)
                sp.dma_start(raw[:, c % RAW_SLOTS, :], wpack[c, :, :]).then_inc(w_in[c % RAW_SLOTS], 16)

            first = C_MERGE + 2 * RAW_SLOTS
            for c in range(first):
                fetch(c)
            sp.wait_ge(s_max, len(UNITS))
            sp.dma_start(xr[:, :, :], x_d.rearrange("(t p) d -> p t d", p=P)).then_inc(xr_in, 16)
            sp.dma_start(wpost[:, :], rows_d[0, :, :]).then_inc(posts_in, 16)
            sp.dma_start(wfpre[:, :], rows_d[1, :, :]).then_inc(posts_in, 16)
            with sp.Fori(0, (N_CHUNKS - first) // RAW_SLOTS) as i:
                for j in range(RAW_SLOTS):
                    c = first + j
                    sp.wait_ge(w_lo_dve, i * RAW_SLOTS + (c - RAW_SLOTS + 1 - C_MERGE))
                    sp.dma_start(raw[:, c % RAW_SLOTS, :],
                                 wpack[bass.ds(i * RAW_SLOTS + c, 1), :, :].rearrange("o p n -> (o p) n")
                                 ).then_inc(w_in[c % RAW_SLOTS], 16)
            for c in range(first + (N_CHUNKS - first) // RAW_SLOTS * RAW_SLOTS, N_CHUNKS):
                fetch(c)
            sp.dma_start(wfpost[:, :], rows_d[2, :, :]).then_inc(wfpost_in, 16)
            for t in range(NT):
                sp.wait_ge(out_ready, t + 1)
                sp.dma_start(out_d[0, t * P:(t + 1) * P, :], x1[:, t, :]).then_inc(stored, 16)
            sp.wait_ge(stored, 16 * NT)

        @block.gpsimd
        def _(pool):
            pool.memset(ident[:, :], 0.0).then_inc(zeros_ready, 1)
            pool.memset(tri[:, :], 1.0 / 16).then_inc(zeros_ready, 1)
            pool.memset(minus_half[:, :], -0.5).then_inc(zeros_ready, 1)
            pool.wait_ge(zeros_ready, 3)
            pool.affine_select(out=ident[:, :], in_=ident[:, :], compare_op=ALU.not_equal, fill=1.0, base=0,
                               pattern=[[-1, P]], channel_multiplier=1).then_inc(const_ready, 1)
            pool.affine_select(out=tri[:, :], in_=tri[:, :], compare_op=ALU.is_ge, fill=0.0, base=0,
                               pattern=[[1, P]], channel_multiplier=-1).then_inc(const_ready, 1)
            pool.memset(attnT[:, :, :, :], 0.0).then_inc(const_ready, 1)
            pool.wait_ge(const_ready, 3)
            zeros = attnT[:, 0:2, :, :].rearrange("p t h c -> p (t h c)")[:, 0:640]
            pool.tensor_copy(ckh[:, :], zeros).then_inc(const_ready, 1)
            pool.tensor_copy(ckl[:, :], zeros).then_inc(const_ready, 1)
            pool.wait_ge(ms_ready, 1)
            pool.tensor_tensor(stat[:, 4:8], stat[:, 0:4], minus_half[:, 0:4], ALU.pow).then_inc(rstd_ready, 1)

            def lo(c):
                s, b = c % RAW_SLOTS, c % SPLIT_SLOTS
                n = WIDTH.get(STRAIGHT[c][0], CHUNK)
                landed(pool, s, c // RAW_SLOTS)
                pool.wait_ge(w_hi, c + 1)
                pool.tensor_tensor(wl[:, b, 0:n], raw[:, s, 0:n], wh[:, b, 0:n].bitcast(F32),
                                   ALU.subtract).then_inc(w_lo_pool, 1)

            def scale(u):
                n = P * (UNITS[u][2] + 1)
                pool.wait_ge(s_rcp, u + 1)
                pool.wait_ge(s_exp, u + 1)
                pool.tensor_tensor(sc[:, u % 8, 0:n], sc[:, u % 8, 0:n],
                                   ast[:, u % 8, 2:3].broadcast_to([P, n]), ALU.mult).then_inc(s_prob, 1)

            lo(0)
            lo(1)
            for c in range(C_MERGE):
                if c + 2 < C_MERGE:
                    lo(c + 2)
                k = c - slot_of("w1k")
                if 0 <= k < NT:
                    pool.wait_ge(o_ms, k + 1)
                    pool.tensor_tensor(stat[:, 32 + 4 * k:36 + 4 * k], stat[:, 16 + 4 * k:20 + 4 * k],
                                       minus_half[:, 0:4], ALU.pow).then_inc(o_rstd, 1)
            for u in range(len(UNITS)):
                scale(u)
            for t in range(NT):
                pool.wait_ge(y_ms, t + 1)
                pool.tensor_tensor(stat[:, 8 + t:9 + t], stat[:, 4 + t:5 + t], minus_half[:, 0:1],
                                   ALU.pow).then_inc(y_rstd, 1)
                pool.wait_ge(x_ms, t + 1)
                pool.tensor_tensor(stat[:, 24 + t:25 + t], stat[:, 20 + t:21 + t], minus_half[:, 0:1],
                                   ALU.pow).then_inc(x_rstd, 1)
            for t in range(NT):
                pool.wait_ge(z_ms, t + 1)
                pool.tensor_tensor(stat[:, 40 + t:41 + t], stat[:, 36 + t:37 + t], minus_half[:, 0:1],
                                   ALU.pow).then_inc(z_rstd, 1)

        @block.scalar
        def _(sa):
            sa.dma_start(onehot[:, :].bitcast(U16), onehot_d[:, :]).then_inc(onehot_in, 16)
            sa.dma_start(lmask[:, :, :], mask_d[:, :, :]).then_inc(mask_in, 16)

            def hi(c):
                s, b = c % RAW_SLOTS, c % SPLIT_SLOTS
                n = WIDTH.get(STRAIGHT[c][0], CHUNK) if c < C_MERGE else CHUNK
                landed(sa, s, c // RAW_SLOTS)
                if c >= SPLIT_SLOTS:
                    sa.wait_ge(w_used, c - SPLIT_SLOTS + 1)
                sa.activation(wh[:, b, 0:n], raw[:, s, 0:n], ACT.Copy).then_inc(w_hi, 1)

            for t in (2, 3):
                sa.wait_ge(x_in[t], 16)
                if t == 3:
                    sa.wait_ge(sq_act, 1)
                sa.activation(gr[:, 0:2, :].rearrange("p a b -> p (a b)"), xs[:, t, :], ACT.Square,
                              accum_out=stat[:, 12 + t:13 + t]).then_inc(sq_act, 1)
            sa.wait_ge(small_in, 16)
            for i in range(10):
                sa.wait_ge(table_full, i + 1)
                ps = bank[i % 8]
                if i < 2:
                    for k in range(2):
                        ins = sa.activation(cmpb[:, 2 * i + k].rearrange("p h n -> p n h"),
                                            ps[:, 256 * k:256 * k + 256].rearrange("p (n h) -> p n h", h=8),
                                            ACT.Copy)
                else:
                    ins = sa.activation(band[:, :, 32 * (i - 2):32 * (i - 1)].rearrange("p h c -> p c h"),
                                        ps[:, :].rearrange("p (c h) -> p c h", h=16), ACT.Copy)
                ins.then_inc(table_out, 1)
            sa.wait_ge(rstd_ready, 1)
            sa.activation(xs[:, 1, :], xs[:, 1, :], ACT.Copy, scale=stat[:, 5:6]).then_inc(xn_act, 1)
            hi(0)
            hi(1)
            for k in range(KD):
                sa.wait_ge(xT_full, k + 1)
                sa.activation(hh[:, k, :], input_bank(k)[:, :], ACT.Copy,
                              scale=small[:, S_PRE + k:S_PRE + k + 1]).then_inc(h_hi, 1)

            def prep_exp(l):
                sa.wait_ge(e_ready, 2 * l + 2)
                sa.activation(zz[:, l % 2, :], zz[:, l % 2, :], ACT.Exp).then_inc(ex_ready, 1)

            for c in range(C_MERGE):
                kind, j = STRAIGHT[c]
                hi(c + 2)
                ps = single_bank(c) if c in SINGLE else None
                done = s_free[SINGLE[c] % 2] if c in SINGLE else None
                if c in SINGLE:
                    sa.wait_ge(w_used, c + 1)
                if kind == "agl":
                    sa.activation(gsq[32:56, :], ps[32:56, :], ACT.Exp, scale=-1.0)
                    sa.activation(gsq[0:16, :], ps[0:16, :], ACT.Copy).then_inc(done, 1)
                elif kind == "bq":
                    sa.activation(gq[:, 512 * j:512 * j + 512], ps[:, :], ACT.Copy, scale=0.125).then_inc(done, 1)
                elif kind == "bk":
                    sa.activation(gk[:, 512 * j:512 * j + 512], ps[:, :], ACT.Copy).then_inc(done, 1)
                elif kind in ("kc", "vc"):
                    kv = 0 if kind == "kc" else 1
                    for odd, g in KX_PARTS:
                        dst, src = kx_part(kxh, ps, kv, odd, g)
                        sa.activation(dst, src, ACT.Copy).then_inc(s_hi, 1)
                    sa.activation(kxh[:, kv, :, 64:68], pe_cols(kv), ACT.Copy).then_inc(pe_col, 1)
                elif kind in ("ks", "kw"):
                    sa.activation(akh[:, 0 if kind == "ks" else 1, :], ps[:, :], ACT.Copy).then_inc(s_hi, 1)
                elif kind in ("aq", "cq"):
                    sa.activation((aqh if kind == "aq" else cqh)[:, j, :], ps[:, :], ACT.Copy,
                                  scale=0.125).then_inc(s_hi, 1)
                elif kind == "ck":
                    sa.activation(kmh[:, j, :], ps[:, :], ACT.Copy).then_inc(s_hi, 1)
                elif kind == "bv" and j == 3:
                    for t in range(NT):
                        tile_done(sa, c, 0, t)
                        sa.activation(gv[:, t, :], bank[t][:, :], ACT.Copy).then_inc(tm_free[t], 1)
                elif kind == "br" and j == 3:
                    for t in range(NT):
                        tile_done(sa, c, 1, t)
                        sa.activation(gr[:, t, :], bank[t][:, :], ACT.Exp, scale=-1.0).then_inc(tm_exp, 1)
                elif kind == "nv" and j == 1:
                    for t in range(NT):
                        tile_done(sa, c, 2, t)
                        sa.activation(av[:, t, :], bank[t][:, 0:256], ACT.Copy).then_inc(tm_free[t], 1)
                elif kind == "cv" and j == 3:
                    for t in range(NT):
                        tile_done(sa, c, 3, t)
                        sa.activation(cv[:, t, :], bank[t][:, :], ACT.Copy).then_inc(tm_free[t], 1)
                if c == 2:
                    aux_out(sa, "z0")
                    aux_out(sa, "z1")
                    sa.activation(zz[:, 0, :], gz[:, :], ACT.Abs).then_inc(softplus, 1)
                    sa.wait_ge(softplus, 1)
                    sa.activation(zz[:, 0, :], zz[:, 0, :], ACT.Exp, scale=-1.0).then_inc(softplus, 1)
                    sa.wait_ge(softplus, 2)
                    sa.activation(zz[:, 0, :], zz[:, 0, :], ACT.Ln, bias=1.0).then_inc(softplus, 1)
                if c == 4:
                    for p in range(2):
                        aux_full(sa, f"bT{p}")
                        sa.activation(bT[:, 512 * p:512 * p + 512], aux_bank(f"bT{p}")[:, :],
                                      ACT.Copy).then_inc(aux_free[AUX_AT[f"bT{p}"] % 2], 1)
                if 5 <= c < 12:
                    prep_exp(c - 5)
                if c == 13:
                    sa.wait_ge(e_ready, 15)
                    sa.activation(zz[:, 0, :], zz[:, 0, :], ACT.Exp).then_inc(ex_ready, 1)
                    aux_full(sa, "lv5_3")
                    sa.activation(zz[:, 1, :], bT[:, :], ACT.Exp).then_inc(ex_ready, 1)
                    sa.activation(ebl[:, :], bT[:, :].rearrange("p (n c) -> p n c", c=P)[:, :, P - 1],
                                  ACT.Exp).then_inc(ex_ready, 1)
                if c == 14:
                    for k in range(2):
                        aux_full(sa, f"kd{k}")
                        sa.activation(gz[:, 512 * k:512 * k + 512], aux_bank(f"kd{k}")[:, :],
                                      ACT.Copy).then_inc(aux_free[AUX_AT[f"kd{k}"] % 2], 1)
                if 15 <= c < 19:
                    t = c - 15
                    aux_full(sa, f"o{t}")
                    if t > 0:
                        sa.wait_ge(o_ms, t)
                    sa.activation(gsq[:, :], aux_bank(f"o{t}")[:, :], ACT.Square).then_inc(o_sq, 1)
                if c == 19:
                    for t in range(NT):
                        sa.wait_ge(ot_full, t + 1)
                        sa.activation(obh[:, :, P * t:P * t + P], bank[t][:, :].rearrange("p (h c) -> p h c", h=4),
                                      ACT.Copy, scale=small[:, S_GNORM:S_GNORM + 1]).then_inc(ot_hi, 1)
                    sa.wait_ge(hid_u, 1)
                    sa.activation(ghid[:, 3, :], ghid[:, 2, :], ACT.Exp, scale=-1.0).then_inc(hid_e, 1)
                if c == FIRST_MOBA - 1:
                    for g in range(2):
                        sa.wait_ge(cs_raw, g + 1)
                        sa.activation(csT[:, g, :], bank[6 + g][:, :], ACT.Copy).then_inc(cs_copied, 1)
                if c == FIRST_MOBA + 1:
                    sa.wait_ge(cs_sub, 1)
                    sa.activation(pcs[:, :, :], pcs[:, :, :], ACT.Exp).then_inc(cs_exp, 1)
                if c == CMP_BACK:
                    for k in range(2):
                        sa.wait_ge(cs_tr, k + 1)
                        sa.activation(pcT[:, 2 * k:2 * k + 2, :].rearrange("p a b -> p (a b)"), bank[6 + k][:, :],
                                      ACT.Copy).then_inc(cs_T, 1)
            attention_act(sa)

            with sa.Fori(0, 4) as i:
                for s in range(6):
                    for part in range(2):
                        c = C_MERGE + 2 * s + 2 + part
                        n = CHUNK if part == 0 or s == 5 else CHUNK // 2
                        if part == 1:
                            sa.wait_ge(w_used, i * 12 + C_MERGE + 2 * s + 1)
                            sa.wait_ge(d_free, i * 6 + s + 1)
                            sa.activation(sig[:, s % 2, :], bank[s % 2][:, :], ACT.Sigmoid).then_inc(d_sig, 1)
                        sa.wait_ge(w_in[c % RAW_SLOTS], i * 48 + 16 * (c // RAW_SLOTS + 1))
                        sa.wait_ge(w_used, i * 12 + c - SPLIT_SLOTS + 1)
                        sa.activation(wh[:, c % 2, 0:n], raw[:, c % RAW_SLOTS, 0:n], ACT.Copy).then_inc(w_hi, 1)
                    if s % 3 == 2:
                        sa.wait_ge(d_acc, i * 4 + 2 * (s // 3) + 2)
                        sa.activation(meh[:, bass.ds(i * 2 + s // 3, 1), :].rearrange("p o n -> p (o n)"),
                                      mrg[:, s // 3, :], ACT.Copy).then_inc(d_mh, 1)
            for m in range(7):
                hi(C_OUT + m + 2)
            for t in range(NT):
                y_tile_done(sa, t)
                for half in range(2):
                    if 2 * t + half + t > 0:
                        sa.wait_ge(y_sq, 2 * t + half)
                    sa.activation(junk[:, :], bank[4 * (1 - half) + t][:, :], ACT.Square,
                                  accum_out=stat[:, 48 + 2 * t + half:49 + 2 * t + half]).then_inc(y_sq, 1)
                sa.wait_ge(x1_ready, t + 1)
                sa.activation(xn[:, t % 2, :], x1[:, t, :], ACT.Square,
                              accum_out=stat[:, 28 + t:29 + t]).then_inc(x_sq, 1)
                if t > 0:
                    transposed_hi(sa, t - 1)
                else:
                    hi(C_OUT + 9)
            transposed_hi(sa, NT - 1)
            with sa.Fori(0, NF // 2) as i:
                for f in range(2):
                    for part in range(2):
                        c = C_FIN + 2 * f + 2 + part
                        if part == 1:
                            sa.wait_ge(w_used, i * 4 + C_FIN + 2 * f + 1)
                            sa.wait_ge(f_free, i * 2 + f + 1)
                            sa.activation(silu[:, f, :], bank[2 * f][:, :], ACT.Silu).then_inc(f_sig, 1)
                        sa.wait_ge(w_in[c % RAW_SLOTS], i * 16 + 16 * (c // RAW_SLOTS + 1))
                        sa.wait_ge(w_used, i * 4 + c - SPLIT_SLOTS + 1)
                        sa.activation(wh[:, c % 2, :], raw[:, c % RAW_SLOTS, :], ACT.Copy).then_inc(w_hi, 1)

            def act_hi(k):
                sa.wait_ge(f_free, k + 3)
                if k >= 2:
                    sa.wait_ge(w_used, C_FOUT + k - 1)
                sa.activation(ash[:, k % 2, :], act[:, k, :], ACT.Copy).then_inc(a_hi, 1)

            for k in range(4):
                act_hi(k)
                if k >= 2:
                    hi(C_FOUT + k)
            with sa.Fori(0, 4) as i:
                for k in range(4, 8):
                    c = C_FOUT + k
                    sa.wait_ge(w_used, i * 4 + c - 1)
                    sa.activation(ash[:, k % 2, :], act[:, bass.ds(i * 4 + k, 1), :].rearrange("p o n -> p (o n)"),
                                  ACT.Copy).then_inc(a_hi, 1)
                    sa.wait_ge(w_in[c % RAW_SLOTS], i * 16 + 16 * (c // RAW_SLOTS + 1))
                    sa.activation(wh[:, c % 2, :], raw[:, c % RAW_SLOTS, :], ACT.Copy).then_inc(w_hi, 1)
            for k in range(20, NF):
                act_hi(k)
                hi(C_FOUT + k)
            for t in range(NT):
                sa.wait_ge(z_full, t + 1)
                for half in range(2):
                    if t + half > 0:
                        sa.wait_ge(z_sq, 2 * t + half)
                    sa.activation(junk[:, :], bank[4 * half + t][:, :], ACT.Square,
                                  accum_out=stat[:, 56 + 2 * t + half:57 + 2 * t + half]).then_inc(z_sq, 1)

        @block.vector
        def _(ve):
            chain = [0]

            def link(ins):
                chain[0] += 1
                ins.then_inc(dchain, 1)
                ve.wait_ge(dchain, chain[0])

            ve.wait_ge(small_in, 16)
            rel = small[0:96, S_REL:S_REL + 16]
            link(ve.tensor_copy(relb[:, 0, :], rel))
            link(ve.tensor_tensor(relr[:, 0, :], rel, relb[:, 0, :], ALU.subtract))
            link(ve.tensor_copy(relb[:, 1, :], relr[:, 0, :]))
            link(ve.tensor_tensor(relr[:, 1, :], relr[:, 0, :], relb[:, 1, :], ALU.subtract))
            link(ve.tensor_copy(relb[:, 2, :], relr[:, 1, :]))
            for k in range(3):
                ve.tensor_copy(rel3[32 * k:32 * k + 32, :], relb[32 * k:32 * k + 32, k, :]).then_inc(rel_ready, 1)
            ve.memset(rel3[96:97, :], MASKED).then_inc(rel_ready, 1)
            for t in range(2):
                ve.wait_ge(x_in[t], 16)
                link(ve.tensor_tensor_reduce(gv[:, 2 * t:2 * t + 2, :].rearrange("p a b -> p (a b)"), xs[:, t, :],
                                             xs[:, t, :], 1.0, 0.0, ALU.mult, ALU.add, stat[:, 12 + t:13 + t]))
            ve.wait_ge(sq_act, 2)
            ve.tensor_scalar(stat[:, 0:4], stat[:, 12:16], 1.0 / D, EPS, ALU.mult, ALU.add).then_inc(ms_ready, 1)
            ve.wait_ge(rstd_ready, 1)
            for t in (0, 2, 3):
                ve.tensor_scalar(xs[:, t, :], xs[:, t, :], stat[:, 4 + t:5 + t], None, ALU.mult).then_inc(xn_ready, 1)
            for k in range(KD):
                ve.wait_ge(h_hi, k + 1)
                ve.scalar_tensor_tensor(out=hl[:, k, :], in0=input_bank(k)[:, :], scalar=small[:, S_PRE + k:S_PRE + k + 1],
                                        in1=hh[:, k, :].bitcast(F32), op0=ALU.mult,
                                        op1=ALU.subtract).then_inc(h_lo, 1)

            def lo(c):
                b = c % SPLIT_SLOTS
                ve.wait_ge(w_hi, c + 1)
                ve.tensor_tensor(wl[:, b, :], raw[:, c % RAW_SLOTS, :], wh[:, b, :].bitcast(F32),
                                 ALU.subtract).then_inc(w_lo_dve, 1)

            def gla_sub(l):
                s = LEVELS[l]
                z, b = level_view(zz[:, l % 2, :], s), level_view(bT[:, :], s)
                n = 512 // s
                if l == 0:
                    ve.wait_ge(ls_ready, 1)
                    aux_out(ve, "bT1")
                    aux_out(ve, "bT0")
                if l >= 2:
                    aux_full(ve, f"lv{l - 2}_3")
                ref = b[:, :, 0, s - 1:s].broadcast_to([P, n, s])
                ve.tensor_tensor(z[:, :, 0, :], ref, b[:, :, 0, :], ALU.subtract).then_inc(e_ready, 1)
                ve.tensor_tensor(z[:, :, 1, :], b[:, :, 1, :], ref, ALU.subtract).then_inc(e_ready, 1)

            def gla_mul(l):
                s = LEVELS[l]
                z = level_view(zz[:, l % 2, :], s)
                ve.wait_ge(ex_ready, l + 1)
                if l == 0:
                    single_out(ve, slot_of("bq", 1))
                    single_out(ve, slot_of("bk", 0))
                    single_out(ve, slot_of("bk", 1))
                ve.tensor_tensor(z[:, :, 0, :], z[:, :, 0, :], level_view(gk[:, :], s)[:, :, 0, :],
                                 ALU.mult).then_inc(z_ready, 1)
                ve.tensor_tensor(z[:, :, 1, :], z[:, :, 1, :], level_view(gq[:, :], s)[:, :, 1, :],
                                 ALU.mult).then_inc(z_ready, 1)

            def gla_pick(l):
                for t in range(NT):
                    aux_full(ve, f"lv{l}_{t}")
                    if l == 0 and t == 0:
                        ve.wait_ge(mask_in, 16)
                        ve.wait_ge(const_ready, 3)
                    if l > 0:
                        aux_out(ve, f"lv{l - 1}_{t}")
                    ve.copy_predicated(attnT[:, t, :, :], lmask[:, l:l + 1, :].broadcast_to([P, 4, P]),
                                       aux_bank(f"lv{l}_{t}")[:, :].rearrange("p (h c) -> p h c", h=4)
                                       ).then_inc(aux_free[AUX_AT[f"lv{l}_{t}"] % 2], 1)

            def silu_r(t):
                ve.wait_ge(tm_exp, t + 1)
                link(ve.tensor_scalar(gr[:, t, :], gr[:, t, :], 1.0, None, ALU.add))
                link(ve.reciprocal(gr[:, t, :], gr[:, t, :]))
                ve.tensor_tensor(gr[:, t, :], gr[:, t, :], bank[t][:, :], ALU.mult).then_inc(tm_free[t], 1)

            for c in range(C_MERGE):
                kind, j = STRAIGHT[c]
                ps = single_bank(c) if c in SINGLE else None
                done = s_free[SINGLE[c] % 2] if c in SINGLE else None
                if kind == "agl":
                    aux_full(ve, "gates")
                    g2 = gate[:, :, :].rearrange("p t g -> p (t g)")
                    ve.tensor_scalar(g2, aux_bank("gates")[:, 0:96], 1.0, None, ALU.add).then_inc(aux_free[0], 1)
                    aux_out(ve, "gates")
                    ve.reciprocal(g2, g2).then_inc(gate_ready, 1)
                elif kind in ("kc", "vc"):
                    kv = 0 if kind == "kc" else 1
                    ve.wait_ge(w_used, c + 1)
                    ve.wait_ge(pe_col, kv + 1)
                    ve.wait_ge(s_hi, 4 * kv + 4)
                    ve.tensor_tensor(kxl[:, kv, :, 64:68], pe_cols(kv), kxh[:, kv, :, 64:68].bitcast(F32),
                                     ALU.subtract)
                    for odd, g in KX_PARTS:
                        dst, src = kx_part(kxl, ps, kv, odd, g)
                        ins = ve.tensor_tensor(dst, src, kx_part(kxh, ps, kv, odd, g)[0].bitcast(F32), ALU.subtract)
                    ins.then_inc(done, 1)
                elif kind in ("w1k", "w1v"):
                    kv = 0 if kind == "w1k" else 1
                    ve.wait_ge(w_used, c + 1)
                    link(ve.tensor_copy(ghid[:, 4, kv:kv + 1], ps[0:64, 64:65]))
                    ve.tensor_scalar(ghid[:, 0, 64 * kv:64 * kv + 64], ps[0:64, 0:64], ghid[:, 4, kv:kv + 1], None,
                                     ALU.add).then_inc(done, 1)
                elif kind in ("ks", "kw", "aq", "cq", "ck"):
                    order = [x for x in STRAIGHT if x[0] in ("ks", "kw", "aq", "cq", "ck")]
                    ve.wait_ge(s_hi, 8 + order.index((kind, j)) + 1)
                    h_, l_ = {"ks": (akh, akl), "kw": (akh, akl), "aq": (aqh, aql), "cq": (cqh, cql),
                              "ck": (kmh, kml)}[kind]
                    k = {"ks": 0, "kw": 1}.get(kind, j)
                    ve.scalar_tensor_tensor(out=l_[:, k, :], in0=ps[:, :],
                                            scalar=0.125 if kind in ("aq", "cq") else 1.0,
                                            in1=h_[:, k, :].bitcast(F32), op0=ALU.mult,
                                            op1=ALU.subtract).then_inc(done, 1)
                if c == 2:
                    for k in range(2):
                        aux_full(ve, f"z{k}")
                        ve.tensor_tensor(gz[:, 512 * k:512 * k + 512].rearrange("p (t n) -> p t n", t=2),
                                         aux_bank(f"z{k}")[:, :].rearrange("p (t n) -> p t n", t=2),
                                         small[:, S_GB:S_GB + 256].unsqueeze(1).broadcast_to([P, 2, 256]),
                                         ALU.add).then_inc(aux_free[AUX_AT[f"z{k}"] % 2], 1)
                    ve.wait_ge(softplus, 3)
                    aux_out(ve, "z0")
                    aux_out(ve, "z1")
                    ve.scalar_tensor_tensor(out=gz[:, :], in0=gz[:, :], scalar=0.0, in1=zz[:, 0, :], op0=ALU.min,
                                            op1=ALU.subtract).then_inc(ls_ready, 1)
                if 5 <= c < 12:
                    gla_sub(c - 5)
                    if c > 5:
                        gla_pick(c - 6)
                    gla_mul(c - 5)
                if c == 12:
                    gla_pick(6)
                if c == 13:
                    b3 = bT[:, :].rearrange("p (n c) -> p n c", c=P)
                    ve.tensor_tensor(zz[:, 0, :].rearrange("p (n c) -> p n c", c=P),
                                     b3[:, :, P - 1:P].broadcast_to([P, 8, P]), b3, ALU.subtract).then_inc(e_ready, 1)
                    gla_pick(7)
                    ve.wait_ge(ex_ready, 10)
                    ve.tensor_tensor(zz[:, 0, :], zz[:, 0, :], gk[:, :], ALU.mult).then_inc(kd_ready, 1)
                    ve.tensor_tensor(zz[:, 1, :], zz[:, 1, :], gq[:, :], ALU.mult).then_inc(kd_ready, 1)
                if 12 <= c < 16:
                    silu_r(c - 12)
                if 15 <= c < 19:
                    t = c - 15
                    if t < 3:
                        aux_full(ve, f"s{t}")
                        ps_s = aux_bank(f"s{t}")[:, :].rearrange("p (a n) -> p a n", a=2)
                        if t == 0:
                            ve.tensor_copy(state[:, :, :], ps_s).then_inc(aux_free[AUX_AT["s0"] % 2], 1)
                        else:
                            aux_out(ve, f"s{t - 1}")
                            link(ve.scalar_tensor_tensor(out=state[:, 0, :], in0=state[:, 0, :],
                                                         scalar=ebl[:, t:t + 1], in1=ps_s[:, 0, :],
                                                         op0=ALU.mult, op1=ALU.add))
                            ve.scalar_tensor_tensor(out=state[:, 1, :], in0=state[:, 1, :],
                                                    scalar=ebl[:, 4 + t:5 + t], in1=ps_s[:, 1, :],
                                                    op0=ALU.mult, op1=ALU.add
                                                    ).then_inc(aux_free[AUX_AT[f"s{t}"] % 2], 1)
                    ve.wait_ge(o_sq, t + 1)
                    link(ve.tensor_reduce(stat[:, 64 + 4 * t:68 + 4 * t],
                                          gsq[:, :].rearrange("p (h c) -> p h c", h=4), AX.X, ALU.add))
                    ve.tensor_scalar(stat[:, 16 + 4 * t:20 + 4 * t], stat[:, 64 + 4 * t:68 + 4 * t], 1.0 / 128, EPS,
                                     ALU.mult, ALU.add).then_inc(o_ms, 1)
                    ve.wait_ge(o_rstd, t + 1)
                    ve.wait_ge(tm_free[t], 2)
                    ps_o = aux_bank(f"o{t}")
                    for h in range(4):
                        ins = ve.scalar_tensor_tensor(out=gr[:, t, P * h:P * h + P], in0=ps_o[:, P * h:P * h + P],
                                                      scalar=stat[:, 32 + 4 * t + h:33 + 4 * t + h],
                                                      in1=gr[:, t, P * h:P * h + P], op0=ALU.mult, op1=ALU.mult)
                    ins.then_inc(aux_free[AUX_AT[f"o{t}"] % 2], 1)
                if c == 19:
                    for t in range(NT):
                        ve.wait_ge(ot_hi, t + 1)
                        ve.scalar_tensor_tensor(out=obl[:, :, P * t:P * t + P],
                                                in0=bank[t][:, :].rearrange("p (h c) -> p h c", h=4),
                                                scalar=small[:, S_GNORM:S_GNORM + 1],
                                                in1=obh[:, :, P * t:P * t + P].bitcast(F32), op0=ALU.mult,
                                                op1=ALU.subtract).then_inc(tm_free[t], 1)
                    single_out(ve, slot_of("w1k"))
                    single_out(ve, slot_of("w1v"))
                    link(ve.tensor_tensor(ghid[:, 1, :], ghid[:, 0, :], ghid[:, 0, :], ALU.mult))
                    link(ve.tensor_scalar(ghid[:, 1, :], ghid[:, 1, :], GELU_3, GELU_1, ALU.mult, ALU.add))
                    link(ve.tensor_tensor(ghid[:, 2, :], ghid[:, 1, :], ghid[:, 0, :], ALU.mult))
                    ve.tensor_scalar(ghid[:, 2, :], ghid[:, 2, :], -80.0, None, ALU.max).then_inc(hid_u, 1)
                    ve.wait_ge(hid_e, 1)
                    link(ve.tensor_scalar(ghid[:, 3, :], ghid[:, 3, :], 1.0, None, ALU.add))
                    link(ve.reciprocal(ghid[:, 3, :], ghid[:, 3, :]))
                    ve.tensor_tensor(ghid[:, 5, :], ghid[:, 3, :], ghid[:, 0, :], ALU.mult).then_inc(hid_ready, 1)
                if c == 20:
                    aux_full(ve, "cmp")
                    ps_c = aux_bank("cmp")
                    for g in range(2):
                        src = ps_c[0:64, 32 * g:32 * g + 32].unsqueeze(1).broadcast_to([64, 4, 32])
                        hi_, lo_ = [m[64 * g:64 * g + 64, :].rearrange("r (p c) -> r p c", p=4)[:, :, 0:32]
                                    for m in (ckh, ckl)]
                        ve.wait_ge(const_ready, 5)
                        link(ve.tensor_copy(hi_, src))
                        link(ve.tensor_tensor(lo_, src, hi_.bitcast(F32), ALU.subtract))
                        for r in range(4):
                            ins = ve.tensor_copy(cvv[32 * r:32 * r + 32, g, :], ps_c[32 * g:32 * g + 32, 64:128])
                            ins.then_inc(cmp_ready, 1)
                if c == FIRST_MOBA:
                    compressed_scores(ve, link)
                if c + 2 >= C_MERGE:
                    lo(c + 2)

            attention_dve(ve, link)
            with ve.Fori(0, 4) as i:
                for s in range(6):
                    for part in range(2):
                        c = C_MERGE + 2 * s + 2 + part
                        n = CHUNK if part == 0 or s == 5 else CHUNK // 2
                        ve.wait_ge(w_hi, i * 12 + c + 1)
                        ve.tensor_tensor(wl[:, c % 2, 0:n], raw[:, c % RAW_SLOTS, 0:n],
                                         wh[:, c % 2, 0:n].bitcast(F32), ALU.subtract).then_inc(w_lo_dve, 1)
                        if part == 0:
                            ve.wait_ge(d_sig, i * 6 + s + 1)
                            ve.wait_ge(w_used, i * 12 + C_MERGE + 2 * s + 2)
                            m, b = mrg[:, s // 3, :], s % 3
                            ve.tensor_tensor(m if b == 0 else prod[:, :], sig[:, s % 2, :], bank[2 + s % 2][:, :],
                                             ALU.mult).then_inc(d_free, 1)
                            if b > 0:
                                ve.wait_ge(d_free, i * 6 + s + 3)
                                if b == 2:
                                    ve.wait_ge(d_acc, i * 4 + 2 * (s // 3) + 1)
                                ve.tensor_tensor(m, m, prod[:, :], ALU.add).then_inc(d_acc, 1)
                    if s % 3 == 2:
                        ve.wait_ge(d_mh, i * 2 + s // 3 + 1)
                        me_n = bass.ds(i * 2 + s // 3, 1)
                        ve.tensor_tensor(mel[:, me_n, :].rearrange("p o n -> p (o n)"), mrg[:, s // 3, :],
                                         meh[:, me_n, :].rearrange("p o n -> p (o n)").bitcast(F32),
                                         ALU.subtract).then_inc(d_ml, 1)

            for m in range(7):
                lo(C_OUT + m + 2)

            def y_mean(t):
                ve.wait_ge(y_sq, 2 * t + 2)
                link(ve.tensor_tensor(stat[:, t:t + 1], stat[:, 48 + 2 * t:49 + 2 * t],
                                      stat[:, 49 + 2 * t:50 + 2 * t], ALU.add))
                ve.tensor_scalar(stat[:, 4 + t:5 + t], stat[:, t:t + 1], 1.0 / D, EPS, ALU.mult,
                                 ALU.add).then_inc(y_ms, 1)

            ve.wait_ge(xr_in, 16)
            ve.wait_ge(posts_in, 32)
            y_mean(0)
            for t in range(NT):
                ve.wait_ge(y_rstd, t + 1)
                for half in range(2):
                    link(ve.scalar_tensor_tensor(out=x1[:, t, 512 * half:512 * half + 512],
                                                 in0=bank[4 * (1 - half) + t][:, :], scalar=stat[:, 8 + t:9 + t],
                                                 in1=wpost[:, 512 * half:512 * half + 512], op0=ALU.mult,
                                                 op1=ALU.mult))
                ve.tensor_tensor(x1[:, t, :], x1[:, t, :], xr[:, t, :], ALU.add).then_inc(x1_ready, 1)
                if t + 1 < NT:
                    y_mean(t + 1)
                ve.wait_ge(x_sq, t + 1)
                ve.tensor_scalar(stat[:, 20 + t:21 + t], stat[:, 28 + t:29 + t], 1.0 / D, EPS, ALU.mult,
                                 ALU.add).then_inc(x_ms, 1)
                if t > 0:
                    transposed_lo(ve, t - 1)
                else:
                    lo(C_OUT + 9)
                ve.wait_ge(x_rstd, t + 1)
                ve.wait_ge(x1_ready, t + 1)
                ve.scalar_tensor_tensor(out=xn[:, t % 2, :], in0=x1[:, t, :], scalar=stat[:, 24 + t:25 + t],
                                        in1=wfpre[:, :], op0=ALU.mult, op1=ALU.mult).then_inc(n_ready, 1)
            transposed_lo(ve, NT - 1)
            ve.engine_nop().then_inc(f_free, 2)
            with ve.Fori(0, NF // 2) as i:
                for f in range(2):
                    for part in range(2):
                        c = C_FIN + 2 * f + 2 + part
                        ve.wait_ge(w_hi, i * 4 + c + 1)
                        ve.tensor_tensor(wl[:, c % 2, :], raw[:, c % RAW_SLOTS, :], wh[:, c % 2, :].bitcast(F32),
                                         ALU.subtract).then_inc(w_lo_dve, 1)
                        if part == 0:
                            ve.wait_ge(f_sig, i * 2 + f + 1)
                            ve.wait_ge(w_used, i * 4 + C_FIN + 2 * f + 2)
                            ve.tensor_tensor(act[:, bass.ds(i * 2 + f, 1), :].rearrange("p o n -> p (o n)"),
                                             silu[:, f, :], bank[2 * f + 1][:, :], ALU.mult).then_inc(f_free, 1)

            def act_lo(k):
                ve.wait_ge(a_hi, k + 1)
                ve.tensor_tensor(asl[:, k % 2, :], act[:, k, :], ash[:, k % 2, :].bitcast(F32),
                                 ALU.subtract).then_inc(a_lo, 1)

            for k in range(4):
                act_lo(k)
                if k >= 2:
                    lo(C_FOUT + k)
            with ve.Fori(0, 4) as i:
                for k in range(4, 8):
                    c = C_FOUT + k
                    ve.wait_ge(a_hi, i * 4 + k + 1)
                    ve.tensor_tensor(asl[:, k % 2, :], act[:, bass.ds(i * 4 + k, 1), :].rearrange("p o n -> p (o n)"),
                                     ash[:, k % 2, :].bitcast(F32), ALU.subtract).then_inc(a_lo, 1)
                    ve.wait_ge(w_hi, i * 4 + c + 1)
                    ve.tensor_tensor(wl[:, c % 2, :], raw[:, c % RAW_SLOTS, :], wh[:, c % 2, :].bitcast(F32),
                                     ALU.subtract).then_inc(w_lo_dve, 1)
            for k in range(20, NF):
                act_lo(k)
                lo(C_FOUT + k)

            def z_mean(t):
                ve.wait_ge(z_sq, 2 * t + 2)
                link(ve.tensor_tensor(stat[:, t:t + 1], stat[:, 56 + 2 * t:57 + 2 * t],
                                      stat[:, 57 + 2 * t:58 + 2 * t], ALU.add))
                ve.tensor_scalar(stat[:, 36 + t:37 + t], stat[:, t:t + 1], 1.0 / D, EPS, ALU.mult,
                                 ALU.add).then_inc(z_ms, 1)

            ve.wait_ge(wfpost_in, 16)
            z_mean(0)
            for t in range(NT):
                ve.wait_ge(z_rstd, t + 1)
                for half in range(2):
                    link(ve.scalar_tensor_tensor(out=xn[:, t % 2, 512 * half:512 * half + 512],
                                                 in0=bank[4 * half + t][:, :], scalar=stat[:, 40 + t:41 + t],
                                                 in1=wfpost[:, 512 * half:512 * half + 512], op0=ALU.mult,
                                                 op1=ALU.mult))
                if t + 1 < NT:
                    z_mean(t + 1)
                ve.tensor_tensor(x1[:, t, :], x1[:, t, :], xn[:, t % 2, :], ALU.add).then_inc(out_ready, 1)

        @block.tensor
        def _(te):
            mm = nc.tensor.matmul

            rows_done = [0]

            def other_rows(ins):
                rows_done[0] += 1
                ins.then_inc(pe_rows, 1)
                te.wait_ge(pe_rows, rows_done[0])

            def three(out, lh, ll, rh, rl, start, stop):
                mm(out, ll, rh, start=start, stop=False, skip_group_check=True)
                mm(out, lh, rl, start=False, stop=False, skip_group_check=True)
                return mm(out, lh, rh, start=False, stop=stop, skip_group_check=True)

            def feature_major(out, b, k0=0, nk=KD, xh=hh, xl=hl):
                for k in range(nk):
                    last = three(out, wh[:, b, k * P:k * P + P], wl[:, b, k * P:k * P + P], xh[:, k, :], xl[:, k, :],
                                 k == 0, k == nk - 1)
                return last

            te.wait_ge(small_in, 16)
            te.wait_ge(onehot_in, 16)
            te.wait_ge(rel_ready, 4)
            for i in range(10):
                if i >= 8:
                    te.wait_ge(table_out, i - 7)
                if i < 2:
                    for k in range(64):
                        t, n = 2 * i + k // 32, k % 32
                        d = P * t - 16 * n - 31 + D0
                        last = mm(bank[i][:, 8 * k:8 * k + 8], onehot[:, d:d + P], rel3[:, 0:8], start=True, stop=True)
                else:
                    for k in range(32):
                        d = P - (32 * (i - 2) + k) + D0
                        last = mm(bank[i % 8][:, 16 * k:16 * k + 16], onehot[:, d:d + P], rel3[:, :],
                                  start=True, stop=True)
                last.then_inc(table_full, 1)
            te.wait_ge(const_ready, 1)
            te.wait_ge(xn_ready, 3)
            te.wait_ge(xn_act, 1)
            te.wait_ge(table_out, 10)
            for k in range(KD):
                for t in range(NT):
                    last = te.transpose(input_bank(k)[:, t * P:t * P + P], xs[:, t, k * P:k * P + P], ident[:, :])
                last.then_inc(xT_full, 1)

            def aux_free_for(name):
                n = AUX_AT[name]
                if n >= 2:
                    te.wait_ge(aux_free[n % 2], n // 2)
                else:
                    te.wait_ge(h_lo, 8)

            def level(l):
                for t in range(NT):
                    name = f"lv{l}_{t}"
                    aux_free_for(name)
                    if l < 7:
                        te.wait_ge(z_ready, 2 * l + 2)
                    for h in (0, 2, 1, 3):
                        b, p = 64 * (h % 2), h // 2
                        if h == 1:
                            other_rows(last)
                        cols = slice(512 * p + P * t, 512 * p + P * t + P)
                        kk = zz[b:b + 64, l % 2, cols] if l < 7 else gk[b:b + 64, cols]
                        qq = zz[b:b + 64, l % 2, cols] if l < 7 else gq[b:b + 64, cols]
                        last = mm(aux_bank(name)[:, P * h:P * h + P], kk, qq, start=True, stop=True)
                    last.then_inc(aux_done, 1)

            def token_major(c):
                kind, j = STRAIGHT[c]
                b = c % 2
                nk, width, n_j = (4, 256, 2) if kind == "nv" else (2, 512, 4)
                for t in range(NT):
                    if j == 0:
                        if TM_USE[kind]:
                            te.wait_ge(tm_free[t], TM_USE[kind])
                    for k in range(nk):
                        cols = slice(k * width, k * width + width)
                        last = three(bank[t][:, 0:width], hh[:, nk * j + k, t * P:t * P + P],
                                     hl[:, nk * j + k, t * P:t * P + P], wh[:, b, cols], wl[:, b, cols],
                                     j == 0 and k == 0, j == n_j - 1 and k == nk - 1)
                    if j == n_j - 1 and t < NT - 1:
                        last.then_inc(tm_done, 1)
                return last

            def chunk(c):
                kind, j = STRAIGHT[c]
                b = c % 2
                te.wait_ge(w_hi, c + 1)
                lo_split(te, c)
                if c in SINGLE:
                    n = SINGLE[c]
                    if n >= 2:
                        te.wait_ge(s_free[n % 2], n // 2)
                if kind == "agl":
                    for k in range(KD):
                        te.wait_ge(h_lo, k + 1)
                        last = three(single_bank(c)[0:64, :], wh[:, b, 64 * k:64 * k + 64],
                                     wl[:, b, 64 * k:64 * k + 64], hh[:, k, :], hl[:, k, :], k == 0, k == KD - 1)
                elif kind in ("bv", "br", "nv", "cv"):
                    last = token_major(c)
                elif kind in ("w1k", "w1v"):
                    kv = 0 if kind == "w1k" else 1
                    single_out(te, slot_of("kc" if kv == 0 else "vc"))
                    for k in range(16):
                        cols = slice(k // 8, k // 8 + 66)
                        last = three(single_bank(c)[0:64, 0:66], wh[:, b, 64 * k:64 * k + 64],
                                     wl[:, b, 64 * k:64 * k + 64], kxh[:, kv, k % 8, cols], kxl[:, kv, k % 8, cols],
                                     k == 0, k == 15)
                else:
                    last = feature_major(single_bank(c)[:, :], b)
                last.then_inc(w_used, 1)

            for c in range(C_MERGE):
                chunk(c)
                if c == 0:
                    te.wait_ge(const_ready, 2)
                    single_out(te, 0)
                    aux_free_for("gates")
                    for t in range(NT):
                        last = te.transpose(aux_bank("gates")[:, 24 * t:24 * t + 24],
                                            gsq[32:56, t * P:t * P + P], ident[32:56, 32:56])
                    last.then_inc(aux_done, 1)
                if c == 2:
                    for t in range(NT):
                        name = f"z{t // 2}"
                        if t % 2 == 0:
                            aux_free_for(name)
                        last = mm(aux_bank(name)[:, 256 * (t % 2):256 * (t % 2) + 256], gsq[0:16, t * P:t * P + P],
                                  small[0:16, S_W2:S_W2 + 256], start=True, stop=True)
                        if t % 2 == 1:
                            last.then_inc(aux_done, 1)
                if c == 4:
                    te.wait_ge(ls_ready, 1)
                    for p in range(2):
                        aux_free_for(f"bT{p}")
                        for t in range(NT):
                            last = mm(aux_bank(f"bT{p}")[:, t * P:t * P + P], gz[:, 256 * t + P * p:256 * t + P * p + P],
                                      tri[:, :], start=True, stop=True)
                        last.then_inc(aux_done, 1)
                if 6 <= c < 14:
                    level(c - 6)
                if c == 14:
                    te.wait_ge(kd_ready, 1)
                    for k in range(2):
                        aux_free_for(f"kd{k}")
                        for t in range(2 * k, 2 * k + 2):
                            for p in range(2):
                                last = te.transpose(aux_bank(f"kd{k}")[:, 256 * (t % 2) + P * p:256 * (t % 2) + P * p + P],
                                                    zz[:, 0, 512 * p + P * t:512 * p + P * t + P], ident[:, :])
                        last.then_inc(aux_done, 1)
                if 15 <= c < 19:
                    t = c - 15
                    aux_free_for(f"o{t}")
                    aux_out(te, f"lv7_{t}")
                    te.wait_ge(kd_ready, 2)
                    te.wait_ge(tm_free[t], 1)
                    if t == 0:
                        aux_out(te, "kd0")
                        aux_out(te, "kd1")
                    else:
                        aux_out(te, f"s{t - 1}")
                    for h in range(4):
                        last = mm(aux_bank(f"o{t}")[:, P * h:P * h + P], attnT[:, t, h, :], gv[:, t, P * h:P * h + P],
                                  start=h == 0, stop=t == 0, skip_group_check=True)
                    for h in (0, 2, 1, 3) if t > 0 else ():
                        b, p = 64 * (h % 2), h // 2
                        if h == 1:
                            other_rows(last)
                        last = mm(aux_bank(f"o{t}")[:, P * h:P * h + P],
                                  zz[b:b + 64, 1, 512 * p + P * t:512 * p + P * t + P],
                                  state[b:b + 64, p, P * (h % 2):P * (h % 2) + P], start=False, stop=True,
                                  skip_group_check=True)
                    last.then_inc(aux_done, 1)
                    if t < 3:
                        aux_free_for(f"s{t}")
                        for p in range(2):
                            last = mm(aux_bank(f"s{t}")[:, 256 * p:256 * p + 256],
                                      gz[:, 256 * t + P * p:256 * t + P * p + P], gv[:, t, 256 * p:256 * p + 256],
                                      start=True, stop=True)
                        last.then_inc(aux_done, 1)
                if c == 19:
                    for t in range(NT):
                        te.wait_ge(tm_free[t], TM_USE["ot"])
                        aux_out(te, f"o{t}")
                        for h in range(4):
                            last = te.transpose(bank[t][:, P * h:P * h + P], gr[:, t, P * h:P * h + P], ident[:, :])
                        last.then_inc(ot_full, 1)
                if c == 20:
                    te.wait_ge(hid_ready, 1)
                    aux_free_for("cmp")
                    ps = aux_bank("cmp")
                    mm(ps[0:64, 0:64], small[0:64, S_CK2:S_CK2 + 64], ghid[:, 5, 0:64], start=True, stop=True)
                    mm(ps[0:64, 64:128], ghid[:, 5, 64:128], small[0:64, S_CV2:S_CV2 + 64], start=True,
                       stop=True).then_inc(aux_done, 1)
                if c == FIRST_MOBA - 1:
                    compressed_scores_pe(te, three)
                if c == FIRST_MOBA:
                    compressed_to_queries(te)
                if c == CMP_BACK:
                    compressed_transposes(te)

            attention_pe(te, mm, three)

            branch = [(oah, oal), (obh, obl), (och, ocl)]
            with te.Fori(0, 4) as i:
                for s in range(6):
                    c = C_MERGE + 2 * s
                    te.wait_ge(d_free, i * 6 + s + 1)
                    te.wait_ge(w_hi, i * 12 + c + 1)
                    te.wait_ge(w_lo_dve, i * 12 + c + 1 - C_MERGE)
                    feature_major(bank[s % 2][:, :], c % 2).then_inc(w_used, 1)
                    te.wait_ge(w_hi, i * 12 + c + 2)
                    te.wait_ge(w_lo_dve, i * 12 + c + 2 - C_MERGE)
                    xh, xl = branch[s % 3]
                    if s % 3 == 0:
                        te.wait_ge(head_lo, 8)
                    if s % 3 == 2:
                        te.wait_ge(head_lo, 16)
                    feature_major(bank[2 + s % 2][:, :], (c + 1) % 2, nk=4, xh=xh, xl=xl).then_inc(w_used, 1)
            te.wait_ge(d_ml, 8)
            for m in range(8):
                c = C_OUT + m
                half, q = m // 4, m % 4
                te.wait_ge(w_hi, c + 1)
                lo_split(te, c)
                if m == 4:
                    te.wait_ge(d_free, 26)
                for t in range(NT):
                    for k in range(2):
                        kk = 2 * q + k
                        cols = slice(512 * k, 512 * k + 512)
                        last = three(bank[4 * (1 - half) + t][:, :], meh[:, kk, t * P:t * P + P],
                                     mel[:, kk, t * P:t * P + P], wh[:, c % 2, cols], wl[:, c % 2, cols],
                                     q == 0 and k == 0, q == 3 and k == 1)
                    if m == 7 and t < NT - 1:
                        last.then_inc(y_full, 1)
                last.then_inc(w_used, 1)
            for t in range(NT):
                te.wait_ge(n_ready, t + 1)
                for half in range(2):
                    for k in range(4):
                        last = te.transpose(bank[4 * half + t][:, k * P:k * P + P],
                                            xn[:, t % 2, (4 * half + k) * P:(4 * half + k) * P + P], ident[:, :])
                    last.then_inc(n_T, 1)
            te.wait_ge(n_lo, 8)
            with te.Fori(0, NF // 2) as i:
                for f in range(2):
                    te.wait_ge(f_free, i * 2 + f + 1)
                    for part in range(2):
                        c = C_FIN + 2 * f + part
                        te.wait_ge(w_hi, i * 4 + c + 1)
                        te.wait_ge(w_lo_dve, i * 4 + c + 1 - C_MERGE)
                        feature_major(bank[2 * f + part][:, :], c % 2).then_inc(w_used, 1)

            def down(k, t, start, stop):
                b, bw = k % 2, (C_FOUT + k) % 2
                for half in range(2):
                    cols = slice(512 * half, 512 * half + 512)
                    last = three(bank[4 * half + t][:, :], ash[:, b, t * P:t * P + P], asl[:, b, t * P:t * P + P],
                                 wh[:, bw, cols], wl[:, bw, cols], start, stop)
                return last

            for k in range(2):
                te.wait_ge(w_hi, C_FOUT + k + 1)
                lo_split(te, C_FOUT + k)
                te.wait_ge(a_hi, k + 1)
                te.wait_ge(a_lo, k + 1)
                if k == 0:
                    te.wait_ge(f_free, NF + 2)
                for t in range(NT):
                    last = down(k, t, k == 0, False)
                last.then_inc(w_used, 1)
            with te.Fori(0, 4) as i:
                for k in range(2, 6):
                    te.wait_ge(w_hi, i * 4 + C_FOUT + k + 1)
                    te.wait_ge(w_lo_dve, i * 4 + C_FOUT + k + 1 - C_MERGE)
                    te.wait_ge(a_hi, i * 4 + k + 1)
                    te.wait_ge(a_lo, i * 4 + k + 1)
                    for t in range(NT):
                        last = down(k, t, False, False)
                    last.then_inc(w_used, 1)
            for k in range(18, 20):
                te.wait_ge(w_hi, C_FOUT + k + 1)
                lo_split(te, C_FOUT + k)
                te.wait_ge(a_hi, k + 1)
                te.wait_ge(a_lo, k + 1)
                for t in range(NT):
                    last = down(k, t, False, False)
                last.then_inc(w_used, 1)
            te.wait_ge(w_hi, N_CHUNKS)
            lo_split(te, N_CHUNKS - 1)
            te.wait_ge(a_hi, NF)
            te.wait_ge(a_lo, NF)
            for t in range(NT):
                down(NF - 2, t, False, False)
                down(NF - 1, t, False, True).then_inc(z_full, 1)



def bucket_of(distance):
    n = np.maximum(distance, 1).astype(np.float32)
    large = 16 + (np.log(n / np.float32(16)) / np.float32(np.log(8.0)) * 16).astype(np.int32)
    return np.where(distance < 16, distance, np.minimum(large, 31))


def distance_onehot():
    d = np.arange(D_TABLE) - D0
    table = np.zeros((97, D_TABLE), np.uint16)
    for k in range(3):
        cols = np.nonzero(d >= 0)[0]
        table[32 * k + bucket_of(d[cols]), cols] = 0x3F80
    table[96, d < 0] = 0x3F80
    return table


def level_masks():
    j, i = np.arange(P)[:, None], np.arange(P)[None, :]
    masks = [(i // (2 * s) == j // (2 * s)) & (j // s % 2 == 0) & (i // s % 2 == 1) for s in LEVELS] + [i == j]
    return np.ascontiguousarray(np.stack(masks, 1).astype(np.uint16))


def pack_weights(a):
    w, out = a["w_in"][0], []
    packed = np.zeros((N_CHUNKS, P, CHUNK), np.float32)

    def tiles(m):
        k, n = m.shape
        return m.reshape(k // P, P, n).transpose(1, 0, 2).reshape(P, k // P * n)

    cols = {"bq": (B_Q, P), "bk": (B_K, P), "kc": (A_KC, P), "vc": (A_VC, P), "ks": (A_KS, P), "kw": (A_KW, P),
            "cq": (C_Q, P), "ck": (C_K, P), }
    for kind, j in STRAIGHT:
        if kind == "agl":
            gap = np.zeros((D, 16), np.float32)
            out.append(tiles(np.concatenate([w[:, B_LR:B_LR + 16], gap, w[:, A_G:A_G + 24], gap[:, :8]], 1)))
        elif kind in cols:
            at, n = cols[kind]
            out.append(tiles(w[:, at + n * j:at + n * j + n]))
        elif kind == "aq":
            out.append(tiles(np.concatenate([w[:, 64 * j:64 * j + 64], w[:, 64 * (j + 4):64 * (j + 4) + 64]], 1)))
        elif kind in ("bv", "br", "cv"):
            at = {"bv": B_V, "br": B_R, "cv": C_V}[kind]
            out.append(tiles(w[256 * j:256 * j + 256, at:at + 512]))
        elif kind == "nv":
            rows = w[512 * j:512 * j + 512]
            out.append(tiles(np.concatenate([rows[:, A_VS:A_VS + P], rows[:, A_VW:A_VW + P]], 1)))
        else:
            m = a["nsa_cmp_k_w1" if kind == "w1k" else "nsa_cmp_v_w1"][0]
            out.append(tiles(m))
    for n in range(KD):
        for b, name in enumerate(("w_branch_a", "w_branch_b", "w_branch_c")):
            out.append(tiles(w[:, M_G + D * b + P * n:M_G + D * b + P * n + P]))
            rows = a[name][0][:, P * n:P * n + P]
            if b == 0:
                rows = rows.reshape(2, 4, 64, P).transpose(1, 0, 2, 3).reshape(512, P)
            out.append(tiles(rows))
    for half in range(2):
        for q in range(4):
            out.append(tiles(a["w_out"][0][256 * q:256 * q + 256, 512 * half:512 * half + 512]))
    for f in range(NF):
        for side in range(2):
            out.append(tiles(a["w_ffn_in"][0][:, HID * side + P * f:HID * side + P * f + P]))
    for k in range(NF):
        out.append(a["w_ffn_out"][0][P * k:P * k + P])
    for c, m in enumerate(out):
        packed[c, :, :m.shape[1]] = m
    return packed


def pack_small(a):
    s = np.zeros((P, S_END), np.float32)
    s[:, S_GNORM] = a["gla_norm"][0]
    s[:, S_GB:S_GB + 256] = a["gla_gate_b"][0][None, :]
    s[0:16, S_W2:S_W2 + 256] = a["gla_gate_w2"][0]
    for k in range(3):
        s[32 * k:32 * k + 32, S_REL:S_REL + 16] = a["rel_bias"]
    for at, name in ((S_PEK, "nsa_pe_k"), (S_PEV, "nsa_pe_v")):
        pe = a[name][0].reshape(2, 8, 2, 64).transpose(2, 3, 1, 0).reshape(P, 8, 2)
        s[:, at:at + 32] = np.concatenate([pe, np.zeros((P, 8, 2), np.float32)], 2).reshape(P, 32)
    s[0:64, S_CK2:S_CK2 + 64] = a["nsa_cmp_k_w2"][0]
    s[0:64, S_CV2:S_CV2 + 64] = a["nsa_cmp_v_w2"][0]
    s[:, S_PRE:S_PRE + KD] = a["norm_mix_pre"][0].reshape(KD, P).T
    return s


def kernel(**inputs):
    import concourse.bacc as bacc
    from concourse.bass_utils import run_bass_kernel_spmd

    a = {k: np.asarray(v) for k, v in inputs.items()}
    rows = np.stack([np.broadcast_to(a[n][0], (P, D)) for n in
                     ("norm_mix_post", "norm_ffn_pre", "norm_ffn_post")])
    arrays = {"wpack": pack_weights(a), "small_params": pack_small(a), "norm_rows": np.ascontiguousarray(rows),
              "distance_onehot": distance_onehot(), "level_masks": level_masks(),
              "x_in": np.ascontiguousarray(a["x"][0])}
    nc = bacc.Bacc("TRN2", target_bir_lowering=False, num_devices=1)
    args = [nc.dram_tensor(n, v.shape, mybir.dt.from_np(v.dtype), kind="ExternalInput").ap()
            for n, v in arrays.items()]
    args.append(nc.dram_tensor("x_out", (1, SEQ, D), F32, kind="ExternalOutput").ap())
    program(nc, *args)
    return run_bass_kernel_spmd(nc, [arrays], core_ids=[0]).results[0]["x_out"]
```
